# Optimizing a Trainium2 kernel written in Bass

```python
import jax, jax.numpy as jnp
from jax import lax
import numpy as np

D_MODEL = 2048
BATCH = 1
SEQ = 512
DEPTH = 1

HEAD_DIM = 128
HEADS_PER_GROUP = 4
DILATED_GROUPS = ((128, 1), (512, 4), (2048, 16))
N_ATTN_HEADS = HEADS_PER_GROUP * len(DILATED_GROUPS)
ATTN_WIDTH = N_ATTN_HEADS * HEAD_DIM
ATTN_OUT_WIDTH = HEADS_PER_GROUP * HEAD_DIM
ATTN_BLOCK = 128
ROPE_THETA = 10000.0
CONV_CHANNELS = D_MODEL // 2
CONV_WIDTH = 31
N_BRANCHES = 2
IN_SPLITS = [ATTN_WIDTH, 2 * ATTN_WIDTH, 3 * ATTN_WIDTH, 3 * ATTN_WIDTH + 2 * CONV_CHANNELS]
IN_COLS = 3 * ATTN_WIDTH + 2 * CONV_CHANNELS + N_BRANCHES * D_MODEL
PEER_HEADS = 8
PEER_N_KEYS = 128
PEER_N_EXPERTS = PEER_N_KEYS * PEER_N_KEYS
PEER_QUERY_DIM = 256
PEER_HALF = PEER_QUERY_DIM // 2
PEER_TOPK = 16
PEER_CHUNK = 128
NORM_EPS = 1e-6
MASK_VALUE = -1e30

kernel_name = 'hybrid_dilated_conformer_peer_block'

def rms_norm(x, gain):
    xf = x.astype(jnp.float32)
    y = xf * lax.rsqrt(jnp.mean(xf * xf, axis=-1, keepdims=True) + NORM_EPS)
    return (y * gain.astype(jnp.float32)).astype(x.dtype)

def layer_norm(x, gain, bias):
    xf = x.astype(jnp.float32)
    mu = jnp.mean(xf, axis=-1, keepdims=True)
    var = jnp.mean(jnp.square(xf - mu), axis=-1, keepdims=True)
    y = (xf - mu) * lax.rsqrt(var + NORM_EPS)
    return (y * gain.astype(jnp.float32) + bias.astype(jnp.float32)).astype(x.dtype)

def rotary(t, positions):
    half = HEAD_DIM // 2
    inv_freq = ROPE_THETA ** (-jnp.arange(0, HEAD_DIM, 2, dtype=jnp.float32) / HEAD_DIM)
    ang = positions.astype(jnp.float32)[..., None] * inv_freq
    cos = jnp.cos(ang)[:, :, None, :]
    sin = jnp.sin(ang)[:, :, None, :]
    tf = t.astype(jnp.float32)
    t1, t2 = tf[..., :half], tf[..., half:]
    return jnp.concatenate([t1 * cos - t2 * sin, t2 * cos + t1 * sin], axis=-1).astype(t.dtype)

def dilated_window_attention(q, k, v, window, dilation):
    B, S, H, Dh = q.shape
    L = S // dilation
    span = window // dilation
    nb = -(-L // ATTN_BLOCK)
    Lp = nb * ATTN_BLOCK

    def to_blocks(t):
        t = t.reshape(B, L, dilation, H, Dh).transpose(0, 2, 1, 3, 4)
        t = jnp.pad(t, ((0, 0), (0, 0), (0, Lp - L), (0, 0), (0, 0)))
        return t.reshape(B, dilation, nb, ATTN_BLOCK, H, Dh)

    def band(t):
        prev = jnp.pad(t, ((0, 0), (0, 0), (1, 0), (0, 0), (0, 0), (0, 0)))[:, :, :-1]
        return jnp.concatenate([prev, t], axis=3)

    qb = to_blocks(q)
    kb = band(to_blocks(k))
    vb = band(to_blocks(v))
    scores = jnp.einsum('brnqhc,brnkhc->brnhqk', qb, kb).astype(jnp.float32) * (Dh ** -0.5)
    qi = jnp.arange(ATTN_BLOCK)[:, None]
    kj = jnp.arange(2 * ATTN_BLOCK)[None, :]
    dist = ATTN_BLOCK + qi - kj
    key_idx = (jnp.arange(nb)[:, None, None] - 1) * ATTN_BLOCK + kj
    valid = (dist >= 0) & (dist <= span) & (key_idx >= 0)
    scores = jnp.where(valid[None, None, :, None], scores, MASK_VALUE)
    lse = jax.nn.logsumexp(scores, axis=-1)
    probs = jnp.exp(scores - lse[..., None]).astype(v.dtype)
    out = jnp.einsum('brnhqk,brnkhc->brnqhc', probs, vb)
    out = out.reshape(B, dilation, Lp, H, Dh)[:, :, :L].transpose(0, 2, 1, 3, 4).reshape(B, S, H, Dh)
    lse = lse.transpose(0, 1, 2, 4, 3).reshape(B, dilation, Lp, H)[:, :, :L]
    lse = lse.transpose(0, 2, 1, 3).reshape(B, S, H)
    return out, lse

def hybrid_mixer(h, positions, w_in, w_attn_o, conv_w, conv_b, conv_ln_g, conv_ln_b, w_conv_o, w_out):
    B, S, _ = h.shape
    proj = h @ w_in
    q, k, v, glu, gates = jnp.split(proj, IN_SPLITS, axis=-1)
    q = rotary(q.reshape(B, S, N_ATTN_HEADS, HEAD_DIM), positions)
    k = rotary(k.reshape(B, S, N_ATTN_HEADS, HEAD_DIM), positions)
    v = v.reshape(B, S, N_ATTN_HEADS, HEAD_DIM)

    outs, lses = [], []
    for g, (window, dilation) in enumerate(DILATED_GROUPS):
        hs = slice(g * HEADS_PER_GROUP, (g + 1) * HEADS_PER_GROUP)
        o, l = dilated_window_attention(q[:, :, hs], k[:, :, hs], v[:, :, hs], window, dilation)
        outs.append(o)
        lses.append(l)
    mix = jax.nn.softmax(jnp.stack(lses, axis=0), axis=0)
    attn = jnp.sum(mix[..., None] * jnp.stack(outs, axis=0).astype(jnp.float32), axis=0)
    attn = attn.astype(h.dtype).reshape(B, S, ATTN_OUT_WIDTH) @ w_attn_o

    a, b = jnp.split(glu, 2, axis=-1)
    u = a * jax.nn.sigmoid(b)
    u = lax.conv_general_dilated(u, conv_w, window_strides=(1,), padding=[(CONV_WIDTH - 1, 0)],
                                 dimension_numbers=('NWC', 'WIO', 'NWC'),
                                 feature_group_count=CONV_CHANNELS) + conv_b
    u = jax.nn.silu(layer_norm(u, conv_ln_g, conv_ln_b))
    conv = u @ w_conv_o

    g_attn, g_conv = jnp.split(jax.nn.sigmoid(gates), N_BRANCHES, axis=-1)
    return (g_attn * attn + g_conv * conv) @ w_out

def peer_ffn(h, w_q, sub_keys, expert_down, expert_up):
    B, S, D = h.shape
    q = (h @ w_q).reshape(B, S, PEER_HEADS, 2, PEER_HALF)
    s1 = jnp.einsum('bshc,hnc->bshn', q[..., 0, :], sub_keys[:, 0]).astype(jnp.float32)
    s2 = jnp.einsum('bshc,hnc->bshn', q[..., 1, :], sub_keys[:, 1]).astype(jnp.float32)
    v1, i1 = lax.top_k(s1, PEER_TOPK)
    v2, i2 = lax.top_k(s2, PEER_TOPK)
    cand = (v1[..., :, None] + v2[..., None, :]).reshape(B, S, PEER_HEADS, PEER_TOPK * PEER_TOPK)
    top, ci = lax.top_k(cand, PEER_TOPK)
    ea = jnp.take_along_axis(i1, ci // PEER_TOPK, axis=-1)
    eb = jnp.take_along_axis(i2, ci % PEER_TOPK, axis=-1)
    expert = ea * PEER_N_KEYS + eb
    gate = jax.nn.softmax(top, axis=-1)

    n_chunks = (B * S) // PEER_CHUNK
    xs = h.reshape(n_chunks, PEER_CHUNK, D)
    idx = expert.reshape(n_chunks, PEER_CHUNK, PEER_HEADS * PEER_TOPK)
    gs = gate.reshape(n_chunks, PEER_CHUNK, PEER_HEADS * PEER_TOPK)

    def chunk(args):
        xc, ic, gc = args
        pre = jnp.einsum('td,tkd->tk', xc, expert_down[ic]).astype(jnp.float32)
        act = jax.nn.gelu(pre, approximate=False) * gc
        return jnp.einsum('tk,tkd->td', act.astype(xc.dtype), expert_up[ic])

    out = lax.map(chunk, (xs, idx, gs))
    return out.reshape(B, S, D)

def setup_inputs(seed: int = 0) -> dict:
    key = jax.random.key(seed)
    ks = jax.random.split(key, 20)
    f32 = jnp.float32
    D = D_MODEL
    nrm = lambda k, shape, scale: jax.random.normal(k, shape, f32) * scale
    return {
        'x': nrm(ks[0], (BATCH, SEQ, D), 1.0),
        'c': nrm(ks[1], (BATCH, D), 1.0),
        'positions': (jnp.arange(SEQ, dtype=jnp.int32)[None, :]
                      + jax.random.randint(ks[2], (BATCH, 1), 0, 4096, dtype=jnp.int32)),
        'ada_w': nrm(ks[3], (DEPTH, D, 6 * D), 0.5 * D ** -0.5),
        'ada_b': nrm(ks[4], (DEPTH, 6 * D), 0.01),
        'norm_gains': 1.0 + nrm(ks[5], (DEPTH, 4, D), 0.05),
        'w_in': nrm(ks[6], (DEPTH, D, IN_COLS), D ** -0.5),
        'w_attn_o': nrm(ks[7], (DEPTH, ATTN_OUT_WIDTH, D), ATTN_OUT_WIDTH ** -0.5),
        'conv_w': nrm(ks[8], (DEPTH, CONV_WIDTH, 1, CONV_CHANNELS), CONV_WIDTH ** -0.5),
        'conv_b': nrm(ks[9], (DEPTH, CONV_CHANNELS), 0.01),
        'conv_ln_g': 1.0 + nrm(ks[10], (DEPTH, CONV_CHANNELS), 0.05),
        'conv_ln_b': nrm(ks[11], (DEPTH, CONV_CHANNELS), 0.01),
        'w_conv_o': nrm(ks[12], (DEPTH, CONV_CHANNELS, D), CONV_CHANNELS ** -0.5),
        'w_out': nrm(ks[13], (DEPTH, D, D), D ** -0.5),
        'peer_w_q': nrm(ks[14], (DEPTH, D, PEER_HEADS * PEER_QUERY_DIM), D ** -0.5),
        'peer_sub_keys': nrm(ks[15], (DEPTH, PEER_HEADS, 2, PEER_N_KEYS, PEER_HALF), PEER_HALF ** -0.5),
        'peer_down': nrm(ks[16], (DEPTH, PEER_N_EXPERTS, D), D ** -0.5),
        'peer_up': nrm(ks[17], (DEPTH, PEER_N_EXPERTS, D), (PEER_HEADS * PEER_TOPK) ** -0.5),
    }

def reference(x, c, positions, ada_w, ada_b, norm_gains, w_in, w_attn_o, conv_w, conv_b,
              conv_ln_g, conv_ln_b, w_conv_o, w_out, peer_w_q, peer_sub_keys, peer_down, peer_up):
    for l in range(DEPTH):
        mod = jax.nn.silu(c) @ ada_w[l] + ada_b[l]
        shift1, scale1, gate1, shift2, scale2, gate2 = jnp.split(mod[:, None, :], 6, axis=-1)
        g = norm_gains[l]
        h = rms_norm(x, g[0]) * (1.0 + scale1) + shift1
        y = hybrid_mixer(h, positions, w_in[l], w_attn_o[l], conv_w[l], conv_b[l],
                         conv_ln_g[l], conv_ln_b[l], w_conv_o[l], w_out[l])
        x = x + gate1 * rms_norm(y, g[1])
        h = rms_norm(x, g[2]) * (1.0 + scale2) + shift2
        y = peer_ffn(h, peer_w_q[l], peer_sub_keys[l], peer_down[l], peer_up[l])
        x = x + gate2 * rms_norm(y, g[3])
    return x


_drawn_inputs = setup_inputs


def setup_inputs(seed=0):
    import zlib

    import numpy as np

    out = dict(_drawn_inputs(seed))
    spreads = {}
    factors = {'conv_ln_b': 3.607}
    for name, (base, spread) in spreads.items():
        noise = np.random.default_rng([zlib.crc32(name.encode()), seed]).standard_normal(out[name].shape)
        drawn = base * np.exp(spread * noise) if base else spread * noise
        out[name] = __import__('jax').numpy.asarray(drawn.astype(out[name].dtype))
    for name, factor in factors.items():
        out[name] = (out[name] * factor).astype(out[name].dtype)
    return out
```

```python
import concourse.bass as bass
from concourse import mybir
from contextlib import ExitStack

D = 2048
S = 512
P = 128
DH = 128
HG = 4
NG = 3
DILATIONS = (1, 4, 16)
AW = NG * HG * DH
AO = HG * DH
CC = D // 2
CW = 31
CO = CC // P
PH = 8
TK = 16
NE = P * P
KT = D // P
TT = S // P
NT = 512
EPS = 1e-6
SCALE = float(DH) ** -0.5
MASK = -1e30
LOWEST = -3.4028235e38
GLU0 = 3 * AW
GATE0 = GLU0 + 2 * CC
UNITS = TT * PH
ROUTE_STEPS = 157
NB = 8


C_ID = 0
C_ONE = C_ID + P
C_M0 = C_ONE + P
C_M1 = C_M0 + TT * 2 * P
C_M2 = C_M1 + P
C_INV = C_M2 + P
C_SGN = C_INV + 1
C_EPS = C_SGN + 1
C_IOTA = C_EPS + 1
C_END = C_IOTA + TK

S_C = 0
S_ADAB = S_C + KT
S_GAIN = S_ADAB + 6 * KT
S_CB = S_GAIN + 4 * KT
S_LG = S_CB + CO
S_LB = S_LG + CO
S_CW = S_LB + CO
S_END = S_CW + CO * CW

TWO_PI = 6.283185307179586
PI = 3.1415925
PI_C1 = 6.28125
PI_C2 = 0.0019350051879882812
PI_C3 = TWO_PI - PI_C1 - PI_C2
ROUND = 12582912.0


def hold(eng, sem, value, passed):
    eng.wait_ge(sem, value)
    if not isinstance(value, int):
        eng.sem_inc(passed, 1)


class Steps:

    def __init__(self, eng, sem, passed):
        self.eng, self.sem, self.n, self.off, self.stack = eng, sem, 0, 0, []
        self.passed = passed

    def did(self, ins):
        ins.then_inc(self.sem, 1)
        self.n += 1
        return self.off + self.n

    def seen(self, value):
        hold(self.eng, self.sem, value, self.passed)

    def link(self, ins):
        self.seen(self.did(ins))

    def enter(self, i, per):
        self.stack.append((self.n, self.off, per))
        self.off = self.off + i * per

    def leave(self, count):
        n, off, per = self.stack.pop()
        assert self.n - n == per, (self.n - n, per)
        self.n, self.off = n + per * count, off


def block_kernel(nc, x, ada_w, w_in, w_attn_o, w_conv_o, w_out, w_q, down, up, keysT, pos, small, const, out):
    fp32 = mybir.dt.float32
    i32 = mybir.dt.int32
    u32 = mybir.dt.uint32
    ALU = mybir.AluOpType
    ACT = mybir.ActivationFunctionType
    AX = mybir.AxisListType.X

    ctx = ExitStack()
    with ctx:
        def sem(name):
            return ctx.enter_context(nc.semaphore(name))

        arena = ctx.enter_context(nc.sbuf_tensor("arena", [P, 52600], fp32))
        psum = ctx.enter_context(nc.psum_tensor("psum", [P, 8 * 512], fp32))
        ps = psum[:, :].rearrange("p (b n) -> p b n", b=8)
        KB = 256

        def view(kb, *dims):
            size = 1
            for d in dims:
                size *= d
            a = arena[:, int(kb * KB):int(kb * KB) + size]
            if len(dims) == 2:
                return a.rearrange("p (a b) -> p a b", a=dims[0])
            if len(dims) == 3:
                return a.rearrange("p (a b c) -> p a b c", a=dims[0], b=dims[1])
            return a

        ring = [view(8 * s, 4, NT) for s in range(4)]
        ring_flat = [view(8 * s, D) for s in range(4)]
        hT = view(32, KT, S)
        xt = view(64, TT, D)
        junk0 = view(32, D)
        mixT = view(64, KT, S)
        sm = [view(64 + 4 * b, TT, 2 * P) for b in range(2)]
        probT = [view(72 + 4 * b, TT * 2, P) for b in range(2)]
        o_sb = view(80, TT, HG * DH + 2 * HG)
        OW = HG * DH + 2 * HG
        og = [view(64 + 6 * t, NG, HG * DH) for t in range(TT)]
        stats = view(94.5, TT, NG, 2 * HG)
        coef = view(95, TT, NG, HG)
        stat_m = view(95.2, TT, HG)
        stat_d = view(95.3, TT, HG)
        cv = view(96, CO, S)
        cosT = view(112, S)
        sinT = view(114, S)
        rt1 = view(116, S)
        rt2 = view(118, S)
        attnT = view(112, HG, S)
        q_sb = view(120, HG, S)
        k_sb = view(128, HG, S)
        v_sb = view(136, TT, HG * DH)
        sga = view(120, HG, S)
        sgc = view(128, HG, S)
        ao_w = view(136, HG, NT)
        UW = S + CW - 1
        u = view(144, CO, UW)
        sig = view(170, HG, S)
        sq = view(144, CO, S)
        co_w = view(144, CO, NT)
        acc = view(161, D)
        ada_ring = [view(169 + 8 * s, D) for s in range(2)]
        cst = view(185, C_END)
        sml = view(192, S_END)
        ident = cst[:, C_ID:C_ID + P]
        ones = cst[:, C_ONE:C_ONE + P]
        mask0 = cst[:, C_M0:C_M0 + TT * 2 * P].rearrange("p (b k) -> p b k", b=TT)
        mask1 = [None, cst[:, C_M1:C_M1 + P], cst[:, C_M2:C_M2 + P]]
        inv_freq = cst[:, C_INV:C_INV + 1]
        sgn = cst[:, C_SGN:C_SGN + 1]
        eps = cst[:, C_EPS:C_EPS + 1]
        iota = cst[:, C_IOTA:C_IOTA + TK]
        sc_w = sml[:, S_CW:S_CW + CO * CW].rearrange("p (c j) -> p c j", c=CO)
        gain = sml[:, S_GAIN:S_GAIN + 4 * KT].rearrange("p (g k) -> p g k", g=4)
        adab = sml[:, S_ADAB:S_ADAB + 6 * KT].rearrange("p (g k) -> p g k", g=6)
        csil = view(194, KT)
        colA = view(194.1, KT)
        colB = view(194.2, KT)
        modc = view(194.3, 4, KT)
        modc_flat = view(194.3, 4 * KT)
        modr = view(194.6, P)
        ssq = view(195.2, 2 * TT)
        std = view(195.3, 2 * TT)
        rstd = view(195.4, 2 * TT)
        ln_std = view(116, S)
        ln_r = view(118, S)
        y_sb = view(32, TT, D)
        rowG1, rowA2, rowB2, rowG3 = (view(96 + 8 * j, D) for j in range(4))
        xb = [view(128 + 8 * b, D) for b in range(2)]
        h2 = view(144, TT, D)
        junk = view(176, D)
        h2T = view(64, KT, S)
        keys = view(96, KT, P)
        qs = view(104, HG, S)
        sc = view(112, HG, TT, P)
        CB = 2 * TT
        v12 = view(32, HG, TT, TK)
        i12 = view(33, HG, TT, TK).bitcast(u32)
        i12f = view(34, HG, TT, TK)
        cand = view(35, CB, TK * TK)
        s2nd = view(43, P)
        cand2 = view(43.5, TK * TK)
        top = view(44.5, CB, TK)
        topi = view(45, CB, TK).bitcast(u32)
        ca = view(45.5, CB, TK).bitcast(u32)
        cb = view(46, CB, TK).bitcast(u32)
        caf = view(46.5, CB, TK)
        cbf = view(47, CB, TK)
        hot = view(47.5, CB * TK, TK)
        ea = view(55.5, CB, TK)
        eb = view(56, CB, TK)
        ex = view(56.5, CB, TK)
        den = view(57, CB)
        rden = view(57.1, CB)
        idx = view(196, UNITS * TK).bitcast(u32)
        gate = view(198, UNITS * TK)
        d_row = [view(8 * s, D) for s in range(NB)]
        u_row = [view(64 + 8 * s, D) if s < 7 else view(128, D) for s in range(NB)]
        zs = view(136, D)
        x2b = view(176, D)
        diag = view(184.5, TK, P)
        ident2 = view(200, P)
        pre = view(200.5, TK)
        gel = view(200.6, TK)
        actv = view(200.7, TK)
        stage = [view(200.8 + 0.1 * s, TK).bitcast(u32) for s in range(3)]
        zq = view(201.2, 4)
        eps2 = view(201.3, 1)
        h2p = psum[:, 0:D]
        zacc = psum[:, D:2 * D]

        scr_o = nc.dram_tensor("attn_parts", [NG, S, OW], fp32, kind="Internal").ap()
        scr_m = nc.dram_tensor("mod_rows", [4, D], fp32, kind="Internal").ap()
        scr_x = nc.dram_tensor("x_after_mixing", [TT, P, D], fp32, kind="Internal").ap()

        consts_in = sem("consts_in")
        passed_waits = sem("passed_waits")
        pos_in = sem("pos_in")
        x_in = [sem(f"x_in{t}") for t in range(TT)]
        ada_in = [sem(f"ada_in{s}") for s in range(4)]
        ada_used = sem("ada_used")
        ada2_in = [sem(f"ada2_in{s}") for s in range(2)]
        ada2_used = sem("ada2_used")
        w_in_sem = [sem(f"w_in{s}") for s in range(4)]
        w_used = sem("w_used")
        ao_in, co_in = sem("ao_in"), sem("co_in")
        csil_ready = sem("csil_ready")
        xn_ready = sem("xn_ready")
        std_ready = sem("std_ready")
        xT_done = sem("xT_done")
        modT_done = sem("modT_done")
        ab_ready = sem("ab_ready")
        hT_ready = sem("hT_ready")
        angle_ready = sem("angle_ready")
        trig_ready = sem("trig_ready")
        proj_done = sem("proj_done")
        sig_ready = sem("sig_ready")
        glu_ready = sem("glu_ready")
        rope_ready = sem("rope_ready")
        v_ready = sem("v_ready")
        s_done = sem("s_done")
        s_read = sem("s_read")
        centred = sem("centred")
        p_ready = sem("p_ready")
        z_ready = sem("z_ready")
        pT_done = sem("pT_done")
        pT_ready = sem("pT_ready")
        pv_done = sem("pv_done")
        o_ready = sem("o_ready")
        o_stored = sem("o_stored")
        stats_in = sem("stats_in")
        og_in = [sem(f"og_in{t}") for t in range(TT)]
        og_used = sem("og_used")
        gap_ready = sem("gap_ready")
        gexp_ready = sem("gexp_ready")
        attnT_done = sem("attnT_done")
        attnT_ready = sem("attnT_ready")
        conv_ready = sem("conv_ready")
        lnsum_done = sem("lnsum_done")
        ln_centred = sem("ln_centred")
        ln_sq = sem("ln_sq")
        lnsq_done = sem("lnsq_done")
        ln_var = sem("ln_var")
        ln_std_ready = sem("ln_std_ready")
        ln_norm = sem("ln_norm")
        convT_ready = sem("convT_ready")
        gate_sig = sem("gate_sig")
        branch_done = sem("branch_done")
        mix_ready = sem("mix_ready")
        adaT_done = sem("adaT_done")
        adaT_read = sem("adaT_read")
        modc_ready = sem("modc_ready")
        modr_done = sem("modr_done")
        modr_ready = sem("modr_ready")
        modr_stored = sem("modr_stored")
        rows_in = sem("rows_in")
        g3_in = sem("g3_in")
        y_ready = sem("y_ready")
        xb_in = [sem(f"xb_in{b}") for b in range(2)]
        ystd_ready = sem("ystd_ready")
        x2_ready = sem("x2_ready")
        x2_stored = [sem(f"x2_stored{b}") for b in range(2)]
        x2std_ready = sem("x2std_ready")
        h2_ready = sem("h2_ready")
        h2T_done = sem("h2T_done")
        h2T_ready = sem("h2T_ready")
        keys_in = sem("keys_in")
        q_ready = sem("q_ready")
        sc_done = sem("sc_done")
        sc_ready = sem("sc_ready")
        sc_used = sem("sc_used")
        gap2_ready = sem("gap2_ready")
        exp2_ready = sem("exp2_ready")
        routed = sem("routed")
        d_in = [sem(f"d_in{s}") for s in range(NB)]
        u_in = [sem(f"u_in{s}") for s in range(NB)]
        staged = sem("staged")
        dots_done = sem("dots_done")
        u_used = sem("u_used")
        h2p_ready = sem("h2p_ready")
        gelu_ready = sem("gelu_ready")
        act_ready = sem("act_ready")
        diag_ready = sem("diag_ready")
        z_read = sem("z_read")
        zstd_ready = sem("zstd_ready")
        x2b_in = sem("x2b_in")
        out_ready = sem("out_ready")
        out_stored = sem("out_stored")
        dve_step, act_step, pool_step = sem("dve_step"), sem("act_step"), sem("pool_step")

        block = ctx.enter_context(nc.Block())

        @block.sync
        def _(sp):
            def ada_load(j, k, s):
                nc.sync.dma_start(ring_flat[s], ada_w[bass.ds(k * P, P), j * D:(j + 1) * D]).then_inc(ada_in[s], 16)

            for s in range(4):
                ada_load(1, s, s)
            with sp.Fori(1, 4) as i:
                for s in range(4):
                    sp.wait_ge(ada_used, 4 * (i - 1) + s + 1)
                    ada_load(1, 4 * i + s, s)
            with sp.Fori(0, 4) as i:
                for s in range(4):
                    sp.wait_ge(ada_used, 4 * (i + 3) + s + 1)
                    ada_load(0, 4 * i + s, s)

            def w_load(G, w, c0, before, first=False):
                for s in range(4):
                    if first:
                        sp.wait_ge(ada_used, 2 * KT - 3 + s)
                    elif s < 3:
                        sp.wait_ge(w_used, 3 * (G - 1) + s + 1)
                    else:
                        hold(sp, proj_done, before, passed_waits)
                    nc.sync.dma_start(ring[s], w[s * NT:(s + 1) * NT, bass.ds(c0, NT)]
                                      .rearrange("(k p) c -> p k c", p=P)).then_inc(w_in_sem[s], 16)

            for i in range(2):
                w_load(2 * i, w_in, GLU0 + CC + i * NT, 8 * i, first=(i == 0))
                w_load(2 * i + 1, w_in, GLU0 + i * NT, 8 * i + 4)
            with sp.Fori(0, NG) as g:
                for part in range(3):
                    w_load(4 + 3 * g + part, w_in, g * NT + part * AW, 4 * (4 + 3 * g + part))

            def branch_load(cg, first):
                w_load(13 + 2 * cg, w_in, GATE0 + cg * NT, 52 if first else 44 + 16 * cg)
                w_load(14 + 2 * cg, w_in, GATE0 + D + cg * NT, 56 + 16 * cg)
                if first:
                    sp.wait_ge(pv_done, NG * HG)
                    sp.wait_ge(lnsq_done, 1)
                else:
                    hold(sp, proj_done, 52 + 16 * cg, passed_waits)
                nc.sync.dma_start(ao_w, w_attn_o[:, bass.ds(cg * NT, NT)].rearrange("(k p) c -> p k c", p=P)).then_inc(ao_in, 16)
                nc.sync.dma_start(co_w, w_conv_o[:, bass.ds(cg * NT, NT)].rearrange("(k p) c -> p k c", p=P)).then_inc(co_in, 16)

            branch_load(0, True)
            with sp.Fori(1, 4) as cg:
                branch_load(cg, False)
            with sp.Fori(0, 4) as n:
                w_load(21 + n, w_out, n * NT, 116 + 4 * n)
            with sp.Fori(0, 4) as n:
                w_load(25 + n, w_q, n * NT, 132 + 4 * n)

            for t in range(TT):
                if t == 0:
                    sp.wait_ge(h2T_ready, 4 * TT)
                    sp.wait_ge(x2std_ready, TT)
                else:
                    sp.wait_ge(out_stored, 16 * t)
                sp.wait_ge(x2_stored[t % 2], 16 * (t // 2 + 1))
                nc.sync.dma_start(x2b, scr_x[t, :, :]).then_inc(x2b_in, 16)
                sp.wait_ge(out_ready, t + 1)
                nc.sync.dma_start(out[t * P:(t + 1) * P, :], zs).then_inc(out_stored, 16)
            sp.wait_ge(out_stored, 16 * TT)

        @block.gpsimd
        def _(pool):
            def ada2(cg, first):
                for k in range(KT):
                    s = k % 2
                    if not (first and k < 2):
                        hold(pool, ada2_used, KT * cg + k - 1, passed_waits)
                    nc.gpsimd.dma_start(ada_ring[s], ada_w[k * P:(k + 1) * P, bass.ds((2 + cg) * D, D)]).then_inc(ada2_in[s], 16)

            pool.wait_ge(glu_ready, 8)
            pool.wait_ge(hT_ready, KT)
            ada2(0, True)
            with pool.Fori(1, 4) as cg:
                ada2(cg, False)

            def gather(table, rows, n, s, into):
                nc.gpsimd.indirect_dma_start(
                    out=rows, out_offset=None, in_=table[:, :],
                    in_offset=bass.IndirectOffsetOnAxis(ap=stage[n][:, s:s + 1], axis=0),
                ).then_inc(into, 16)

            def put_stage(n, b, first=False):
                if not first:
                    hold(pool, u_used, TK * (n - 2) + 1, passed_waits)
                nc.gpsimd.tensor_copy(stage[b], idx[:, bass.ds(n * TK, TK)]).then_inc(staged, 1)
                hold(pool, staged, n + 1, passed_waits)

            def down_row(n, b, s, first=False):
                if not (first and s < NB):
                    hold(pool, dots_done, TK * n + s - NB + 1, passed_waits)
                gather(down, d_row[s % NB], b, s, d_in[s % NB])

            def up_row(n, b, s, first=False):
                if not (first and s < NB):
                    hold(pool, u_used, TK * n + s - NB + 1, passed_waits)
                gather(up, u_row[s % NB], b, s, u_in[s % NB])

            pool.wait_ge(routed, 4)
            for b in range(2):
                pool.wait_ge(x2_stored[b], 32)
            pool.wait_ge(q_ready, KT)
            pool.wait_ge(sc_done, KT)
            put_stage(0, 0, first=True)
            for s in range(TK):
                down_row(0, 0, s, first=True)
            put_stage(1, 1, first=True)
            for s in range(TK):
                down_row(1, 1, s)
                up_row(0, 0, s, first=True)
            with pool.Fori(0, 10) as j:
                for p in range(3):
                    i = 3 * j + (p + 1)
                    put_stage(i + 1, (p + 2) % 3)
                    for s in range(TK):
                        down_row(i + 1, (p + 2) % 3, s)
                        up_row(i, (p + 1) % 3, s)
            for s in range(TK):
                up_row(UNITS - 1, (UNITS - 1) % 3, s)

        @block.tensor
        def _(pe):
            def mm(o, a, b, start, stop):
                return nc.tensor.matmul(o, a, b, start=start, stop=stop)

            pe.wait_ge(consts_in, 32)
            def transpose_x(k):
                for t in range(TT):
                    ins = nc.tensor.transpose(ps[:, k % 6, t * P:(t + 1) * P], xt[:, t, k * P:(k + 1) * P], ident)
                ins.then_inc(xT_done, 1)

            def mod_columns(bank):
                for k in range(KT):
                    ins = mm(ps[:, bank, k:k + 1], acc[:, k * P:(k + 1) * P], ones[:, 0:1], True, True)
                return ins

            pe.wait_ge(xn_ready, TT)
            for k in range(6):
                transpose_x(k)
            for j in range(2):
                pe.wait_ge(ada_used, KT * (j + 1))
                mod_columns(6 + j).then_inc(modT_done, 1)
            for k in range(6, KT):
                pe.wait_ge(hT_ready, k - 5)
                transpose_x(k)

            def project(G, half, rhs):
                for s in range(4):
                    pe.wait_ge(w_in_sem[s], 16 * (G + 1))
                    for m in range(4):
                        for k in range(4):
                            ins = mm(ps[:, 4 * half + m, :], ring[s][:, k, m * P:(m + 1) * P], rhs[:, 4 * s + k, :],
                                     s == 0 and k == 0, s == 3 and k == 3)
                        if s == 3:
                            ins.then_inc(proj_done, 1)
                    if s < 3:
                        ins.then_inc(w_used, 1)

            def project_tokens(G, half, lhs):
                for s in range(4):
                    pe.wait_ge(w_in_sem[s], 16 * (G + 1))
                    for t in range(TT):
                        for k in range(4):
                            ins = mm(ps[:, 4 * half + t, :], lhs(4 * s + k, t), ring[s][:, k, :],
                                     s == 0 and k == 0, s == 3 and k == 3)
                        if s == 3:
                            ins.then_inc(proj_done, 1)
                    if s < 3:
                        ins.then_inc(w_used, 1)

            pe.wait_ge(hT_ready, KT)
            for i in range(2):
                if i:
                    pe.wait_ge(sig_ready, 4)
                project(2 * i, 1, hT)
                if i:
                    pe.wait_ge(glu_ready, 4)
                project(2 * i + 1, 0, hT)

            for g, dil in enumerate(DILATIONS):
                if g == 0:
                    pe.wait_ge(sig_ready, 8)
                project(4 + 3 * g, 1, hT)
                if g == 0:
                    pe.wait_ge(glu_ready, 8)
                project(5 + 3 * g, 0, hT)
                pe.wait_ge(rope_ready, 8 * g + 4)

                def tokens(k, t):
                    if dil == 1:
                        return hT[:, k, t * P:(t + 1) * P]
                    return hT[:, k, :].rearrange("p (l r) -> p r l", r=TT)[:, t, :]

                project_tokens(6 + 3 * g, 1, tokens)
                pe.wait_ge(rope_ready, 8 * g + 8)

                def scores(h):
                    H = HG * g + h
                    if h >= 2:
                        pe.wait_ge(s_read, H - 1)
                    S_ = psum[:, 1024 * (h % 2):1024 * (h % 2) + 1024].rearrange("p (b k) -> p b k", b=TT)
                    for b in range(TT):
                        qb = q_sb[:, h, b * P:(b + 1) * P]
                        if g == 0:
                            pb = max(b - 1, 0)
                            mm(S_[:, b, 0:P], qb, k_sb[:, h, pb * P:(pb + 1) * P], True, True)
                        ins = mm(S_[:, b, P:2 * P], qb, k_sb[:, h, b * P:(b + 1) * P], True, True)
                    ins.then_inc(s_done, 1)

                def turn(h):
                    H = HG * g + h
                    pe.wait_ge(p_ready, H + 1)
                    if h == 0:
                        pe.wait_ge(v_ready, TT * (g + 1))
                    else:
                        pe.wait_ge(pT_ready, H)
                    T_ = psum[:, 2048:3072].rearrange("p (b k) -> p b k", b=8)
                    for b in range(TT):
                        for half in ((0, 1) if g == 0 and b else (1,)):
                            ins = nc.tensor.transpose(T_[:, 2 * b + half, :], sm[h % 2][:, b, half * P:(half + 1) * P], ident)
                    ins.then_inc(pT_done, 1)

                def values(h):
                    H = HG * g + h
                    pe.wait_ge(pT_ready, H + 1)
                    if h >= 2:
                        pe.wait_ge(o_ready, H - 1)
                    for b in range(TT):
                        prev = g == 0 and b > 0
                        o = ps[:, 6 + h % 2, b * DH:(b + 1) * DH]
                        if prev:
                            mm(o, probT[h % 2][:, 2 * b, :], v_sb[:, b - 1, h * DH:(h + 1) * DH], True, False)
                        ins = mm(o, probT[h % 2][:, 2 * b + 1, :], v_sb[:, b, h * DH:(h + 1) * DH], not prev, True)
                    ins.then_inc(pv_done, 1)

                scores(0)
                scores(1)
                for h in range(HG):
                    turn(h)
                    values(h)
                    if h + 2 < HG:
                        scores(h + 2)
                pe.wait_ge(o_ready, HG * (g + 1))
                pe.wait_ge(s_read, HG * (g + 1))

            pe.wait_ge(conv_ready, CO)
            for c in range(CO):
                ins = mm(ps[:, 7, :], ones, cv[:, c, :], c == 0, c == CO - 1)
            ins.then_inc(lnsum_done, 1)

            def branches(cg, first):
                if not first:
                    pe.wait_ge(branch_done, 8 * cg)
                project(13 + 2 * cg, 0, hT)
                if first:
                    pe.wait_ge(ln_centred, CO)
                    for c in range(CO):
                        pe.wait_ge(ln_sq, c + 1)
                        ins = mm(ps[:, 7, :], ones, sq[:, c, :], c == 0, c == CO - 1)
                    ins.then_inc(lnsq_done, 1)
                    pe.wait_ge(ln_var, 1)
                project(14 + 2 * cg, 1, hT)
                pe.wait_ge(gate_sig, 8 * cg + 4)
                if first:
                    for t in range(TT):
                        pe.wait_ge(og_used, HG * NG * (t + 1))
                        for h in range(HG):
                            ins = nc.tensor.transpose(ps[:, t, h * P:(h + 1) * P], og[t][:, 0, h * P:(h + 1) * P], ident)
                        ins.then_inc(attnT_done, 1)
                    pe.wait_ge(attnT_ready, TT)
                pe.wait_ge(ao_in, 16 * (cg + 1))
                for m in range(4):
                    for k in range(HG):
                        ins = mm(ps[:, m, :], ao_w[:, k, m * P:(m + 1) * P], attnT[:, k, :], k == 0, k == HG - 1)
                    ins.then_inc(proj_done, 1)
                pe.wait_ge(gate_sig, 8 * cg + 8)
                pe.wait_ge(ada2_used, KT * (cg + 1))
                mod_columns(4).then_inc(adaT_done, 1)
                pe.wait_ge(adaT_read, cg + 1)
                pe.wait_ge(co_in, 16 * (cg + 1))
                if first:
                    pe.wait_ge(convT_ready, CO)
                for m in range(4):
                    for k in range(CO):
                        ins = mm(ps[:, 4 + m, :], co_w[:, k, m * P:(m + 1) * P], cv[:, k, :], k == 0, k == CO - 1)
                    ins.then_inc(proj_done, 1)

            branches(0, True)
            with pe.Fori(1, 4) as cg:
                branches(cg, False)

            pe.wait_ge(branch_done, 32)
            pe.wait_ge(modc_ready, 1)
            nc.tensor.transpose(ps[0:4 * KT, 0, 0:P], modc_flat, ident).then_inc(modr_done, 1)
            pe.wait_ge(modr_ready, 1)

            def mixed(k, t):
                return mixT[:, k, t * P:(t + 1) * P]

            pe.wait_ge(mix_ready, KT)
            project_tokens(21, 0, mixed)
            project_tokens(22, 1, mixed)
            for half in range(2):
                pe.wait_ge(y_ready, 4 * half + 4)
                project_tokens(23 + half, half, mixed)

            for t in range(TT):
                pe.wait_ge(h2_ready, t + 1)
                if t == 0:
                    pe.wait_ge(y_ready, 16)
                for k4 in range(4):
                    if t >= 2:
                        pe.wait_ge(h2T_ready, 4 * (t - 2) + k4 + 1)
                    for k in range(4):
                        ins = nc.tensor.transpose(ps[:, 4 * (t % 2) + k4, k * P:(k + 1) * P],
                                                  h2[:, t, (4 * k4 + k) * P:(4 * k4 + k + 1) * P], ident)
                    ins.then_inc(h2T_done, 1)

            pe.wait_ge(h2T_ready, 4 * TT)
            pe.wait_ge(keys_in, 16)
            def route_products(n, first=False):
                project(25 + n, 0, h2T)
                for m in range(4):
                    pe.wait_ge(q_ready, 4 * n + m + 1)
                    if not first:
                        pe.wait_ge(sc_ready, 4 * n)
                    for t in range(TT):
                        ins = mm(ps[:, 4 + m, t * P:(t + 1) * P], qs[:, m, t * P:(t + 1) * P],
                                 keys[:, bass.ds(4 * n + m, 1), :], True, True)
                    ins.then_inc(sc_done, 1)

            route_products(0, True)
            with pe.Fori(1, 4) as n:
                route_products(n)

            def unit(n, first, last):
                for s in range(TK):
                    pe.wait_ge(diag_ready, TK * n + s + 1)
                    pe.wait_ge(u_in[s % NB], 16 * (2 * n + s // NB + 1))
                    for c in range(4):
                        ins = mm(zacc[:, c * 512:(c + 1) * 512], diag[:, s, :], u_row[s % NB][:, c * 512:(c + 1) * 512],
                                 first and s == 0, last and s == TK - 1)
                    ins.then_inc(u_used, 1)

            pe.wait_ge(sc_ready, KT)

            def tile(t):
                unit(PH * t, True, False)
                with pe.Fori(1, PH - 1) as h:
                    unit(PH * t + h, False, False)
                unit(PH * t + (PH - 1), False, True)

            tile(0)
            with pe.Fori(1, TT) as t:
                pe.wait_ge(z_read, t)
                tile(t)

        @block.scalar
        def _(act):
            st = Steps(act, act_step, passed_waits)
            A = nc.scalar.activation
            nc.scalar.dma_start(sml, small).then_inc(consts_in, 16)
            nc.scalar.dma_start(cst, const).then_inc(consts_in, 16)
            nc.scalar.dma_start(cosT.bitcast(i32), pos[0:1, :].to_broadcast([P, S])).then_inc(pos_in, 16)
            for t in range(TT):
                nc.scalar.dma_start(xt[:, t, :], x[t * P:(t + 1) * P, :]).then_inc(x_in[t], 16)
            act.wait_ge(consts_in, 32)
            A(csil, sml[:, S_C:S_C + KT], ACT.Silu).then_inc(csil_ready, 1)
            for t in range(TT):
                act.wait_ge(x_in[t], 16)
                st.link(A(junk0, xt[:, t, :], ACT.Square, accum_out=ssq[:, t:t + 1]))
            A(std[:, 0:TT], ssq[:, 0:TT], ACT.Sqrt, scale=1.0 / D, bias=eps).then_inc(std_ready, 1)
            act.wait_ge(angle_ready, 1)
            A(sinT, rt1, ACT.Sin).then_inc(trig_ready, 1)
            A(cosT, rt2, ACT.Sin).then_inc(trig_ready, 1)

            act.wait_ge(ab_ready, 1)
            for k in range(KT):
                act.wait_ge(xT_done, k + 1)
                A(hT[:, k, :], ps[:, k % 6, :], ACT.Identity, scale=colA[:, k:k + 1], bias=colB[:, k:k + 1]).then_inc(hT_ready, 1)

            for i in range(2):
                for m in range(4):
                    act.wait_ge(proj_done, 8 * i + m + 1)
                    if i:
                        act.wait_ge(glu_ready, m + 1)
                    A(sig[:, m, :], ps[:, 4 + m, :], ACT.Sigmoid).then_inc(sig_ready, 1)

            for g in range(NG):
                W0 = 0 if g == 0 else P
                for t in range(TT):
                    act.wait_ge(proj_done, 16 + 12 * g + 8 + t + 1)
                    if g:
                        act.wait_ge(pv_done, HG * g)
                    A(v_sb[:, t, :], ps[:, 4 + t, :], ACT.Copy).then_inc(v_ready, 1)

                def exps(h):
                    H = HG * g + h
                    act.wait_ge(centred, H + 1)
                    A(sm[h % 2][:, :, W0:], sm[h % 2][:, :, W0:], ACT.Exp).then_inc(p_ready, 1)

                exps(0)
                for h in range(HG):
                    H = HG * g + h
                    act.wait_ge(pT_done, H + 1)
                    if H >= 2:
                        act.wait_ge(pv_done, H - 1)
                    T_ = psum[:, 2048:3072].rearrange("p (b k) -> p b k", b=8)
                    if g == 0:
                        A(probT[h % 2][:, 1:, :], T_[:, 1:, :], ACT.Copy).then_inc(pT_ready, 1)
                    else:
                        odd = T_.rearrange("p (b two) k -> p b two k", two=2)[:, :, 1, :]
                        A(probT[h % 2].rearrange("p (b two) k -> p b two k", two=2)[:, :, 1, :], odd, ACT.Copy).then_inc(pT_ready, 1)
                    if h + 1 < HG:
                        exps(h + 1)
                    act.wait_ge(pv_done, H + 1)
                    if g and h == 0:
                        act.wait_ge(o_stored, 16 * TT * g)
                    A(o_sb[:, :, h * DH:(h + 1) * DH], ps[:, 6 + h % 2, :].rearrange("p (b d) -> p b d", b=TT), ACT.Copy).then_inc(o_ready, 1)
                act.wait_ge(o_ready, HG * (g + 1))
                act.wait_ge(z_ready, HG * (g + 1))
                for b in range(TT):
                    rows = scr_o[g, b * P:(b + 1) * P, :] if g == 0 else scr_o[g].rearrange("(l r) c -> r l c", r=TT)[b]
                    nc.scalar.dma_start(rows, o_sb[:, b, :]).then_inc(o_stored, 16)

            act.wait_ge(o_stored, 16 * TT * NG)
            for g in range(NG):
                nc.scalar.dma_start(stats[:, :, g, :], scr_o[g].rearrange("(t p) c -> p t c", p=P)[:, :, HG * DH:]).then_inc(stats_in, 16)

            for t in range(TT):
                nc.scalar.dma_start(og[t], scr_o[:, t * P:(t + 1) * P, 0:HG * DH].rearrange("g p c -> p g c")).then_inc(og_in[t], 16)
            act.wait_ge(gap_ready, NG)
            A(coef, coef, ACT.Exp).then_inc(gexp_ready, 1)

            for c in range(CO):
                act.wait_ge(ln_centred, c + 1)
                A(sq[:, c, :], cv[:, c, :], ACT.Square).then_inc(ln_sq, 1)

            def branch_gates(cg, first):
                for m in range(4):
                    act.wait_ge(proj_done, 52 + 16 * cg + m + 1)
                    if not first:
                        act.wait_ge(mix_ready, 4 * cg)
                    A(sga[:, m, :], ps[:, m, :], ACT.Sigmoid).then_inc(gate_sig, 1)
                if first:
                    act.wait_ge(ln_var, 1)
                    A(ln_std, ln_std, ACT.Sqrt).then_inc(ln_std_ready, 1)
                    for c in range(CO):
                        act.wait_ge(ln_norm, c + 1)
                        A(cv[:, c, :], cv[:, c, :], ACT.Silu, scale=sml[:, S_LG + c:S_LG + c + 1],
                          bias=sml[:, S_LB + c:S_LB + c + 1]).then_inc(convT_ready, 1)
                for m in range(4):
                    act.wait_ge(proj_done, 52 + 16 * cg + 4 + m + 1)
                    A(sgc[:, m, :], ps[:, 4 + m, :], ACT.Sigmoid).then_inc(gate_sig, 1)
                if first:
                    for t in range(TT):
                        act.wait_ge(attnT_done, t + 1)
                        A(attnT[:, :, t * P:(t + 1) * P], ps[:, t, :].rearrange("p (h d) -> p h d", h=HG), ACT.Copy).then_inc(attnT_ready, 1)
                act.wait_ge(adaT_done, cg + 1)
                A(modc[:, bass.ds(cg, 1), :], ps[:, 4, 0:KT], ACT.Copy).then_inc(adaT_read, 1)

            branch_gates(0, True)
            with act.Fori(1, 4) as cg:
                branch_gates(cg, False)

            act.wait_ge(modr_done, 1)
            A(modr[0:4 * KT, :], ps[0:4 * KT, 0, 0:P], ACT.Copy).then_inc(modr_ready, 1)
            act.wait_ge(modr_ready, 1)
            nc.scalar.dma_start(scr_m.rearrange("j (k c) -> (j k) c", c=P), modr[0:4 * KT, :]).then_inc(modr_stored, 16)
            act.wait_ge(modr_stored, 16)
            act.wait_ge(mix_ready, KT)
            act.wait_ge(proj_done, 116)
            for j, row in enumerate((rowG1, rowB2, rowA2)):
                nc.scalar.dma_start(row, scr_m[j:j + 1, :].to_broadcast([P, D])).then_inc(rows_in, 16)
            nc.scalar.dma_start(rowG3, scr_m[3:4, :].to_broadcast([P, D])).then_inc(g3_in, 16)

            def x_load(t):
                if t >= 2:
                    act.wait_ge(x2_stored[t % 2], 16)
                    act.wait_ge(h2_ready, t - 1)
                nc.scalar.dma_start(xb[t % 2], x[t * P:(t + 1) * P, :]).then_inc(xb_in[t % 2], 16)

            x_load(0)
            x_load(1)
            with act.Fori(0, 2) as i:
                for half in range(2):
                    for t in range(TT):
                        act.wait_ge(proj_done, 116 + 8 * i + 4 * half + t + 1)
                        A(y_sb[:, t, bass.ds((2 * i + half) * NT, NT)], ps[:, 4 * half + t, :], ACT.Copy).then_inc(y_ready, 1)

            act.wait_ge(y_ready, 16)

            def y_std(t):
                st.link(A(junk, y_sb[:, t, :], ACT.Square, accum_out=ssq[:, t:t + 1]))
                A(std[:, t:t + 1], ssq[:, t:t + 1], ACT.Sqrt, scale=1.0 / D, bias=eps).then_inc(ystd_ready, 1)

            def h2T_out(t):
                for k4 in range(4):
                    act.wait_ge(h2T_done, 4 * t + k4 + 1)
                    A(h2T[:, 4 * k4:4 * k4 + 4, t * P:(t + 1) * P],
                      ps[:, 4 * (t % 2) + k4, :].rearrange("p (k c) -> p k c", k=4), ACT.Copy).then_inc(h2T_ready, 1)

            act.wait_ge(ada2_used, 4 * KT)
            act.wait_ge(std_ready, 1)
            y_std(0)
            for t in range(TT):
                act.wait_ge(x2_ready, t + 1)
                nc.scalar.dma_start(scr_x[t, :, :], xb[t % 2]).then_inc(x2_stored[t % 2], 16)
                st.link(A(junk, xb[t % 2], ACT.Square, accum_out=ssq[:, TT + t:TT + t + 1]))
                A(std[:, TT + t:TT + t + 1], ssq[:, TT + t:TT + t + 1], ACT.Sqrt, scale=1.0 / D, bias=eps).then_inc(x2std_ready, 1)
                if t + 1 < TT:
                    y_std(t + 1)
                if t + 2 < TT:
                    x_load(t + 2)
                if t:
                    h2T_out(t - 1)
            act.wait_ge(h2_ready, TT)
            nc.scalar.dma_start(keys.rearrange("p k c -> p (k c)"), keysT).then_inc(keys_in, 16)
            h2T_out(TT - 1)

            def route_copies(n, first=False):
                for m in range(4):
                    act.wait_ge(proj_done, 132 + 4 * n + m + 1)
                    if not first:
                        act.wait_ge(sc_done, 4 * n)
                    A(qs[:, m, :], ps[:, m, :], ACT.Copy).then_inc(q_ready, 1)
                for m in range(4):
                    act.wait_ge(sc_done, 4 * n + m + 1)
                    if not first:
                        act.wait_ge(sc_used, n)
                    A(sc[:, m, :, :], ps[:, 4 + m, :].rearrange("p (t k) -> p t k", t=TT), ACT.Copy).then_inc(sc_ready, 1)
                act.wait_ge(gap2_ready, n + 1)
                A(ex, ex, ACT.Exp).then_inc(exp2_ready, 1)

            route_copies(0, True)
            with act.Fori(1, 4) as n:
                route_copies(n)

            st.link(A(ident2, ident, ACT.Copy))
            act.wait_ge(sc_used, 4)
            act.wait_ge(q_ready, KT)
            act.wait_ge(sc_ready, KT)

            def load_h2p(t):
                A(h2p, h2[:, bass.ds(t, 1), :], ACT.Copy).then_inc(h2p_ready, 1)

            def unit(n, first=False):
                act.wait_ge(dots_done, TK * n + TK)
                A(gel, pre, ACT.Gelu).then_inc(gelu_ready, 1)
                act.wait_ge(act_ready, n + 1)
                for s in range(TK):
                    if not first:
                        act.wait_ge(u_used, TK * (n - 1) + s + 1)
                    A(diag[:, s, :], ident2, ACT.Copy, scale=actv[:, s:s + 1]).then_inc(diag_ready, 1)

            def take_z(t):
                act.wait_ge(u_used, TK * PH * (t + 1))
                act.wait_ge(x2b_in, 16 * (t + 1))
                A(zs, zacc, ACT.Copy)
                A(zacc, zacc, ACT.Square, accum_out=zq[:, 0:1]).then_inc(z_read, 1)
                act.wait_ge(z_read, t + 1)
                A(zq[:, 1:2], zq[:, 0:1], ACT.Sqrt, scale=1.0 / D, bias=eps2).then_inc(zstd_ready, 1)

            for b in range(2):
                act.wait_ge(x2_stored[b], 32)
            A(eps2, eps, ACT.Copy)
            load_h2p(0)
            unit(0, True)
            with act.Fori(1, PH) as h:
                unit(h)
            with act.Fori(1, TT) as t:
                act.wait_ge(dots_done, TK * PH * t)
                load_h2p(t)
                unit(PH * t)
                take_z(t - 1)
                with act.Fori(1, PH) as h:
                    unit(PH * t + h)
            take_z(TT - 1)

        @block.vector
        def _(dve):
            st = Steps(dve, dve_step, passed_waits)
            V = nc.vector
            dve.wait_ge(consts_in, 32)
            dve.wait_ge(pos_in, 16)
            st.link(V.tensor_copy(rt1, cosT.bitcast(i32)))
            st.link(V.tensor_scalar(rt1, rt1, inv_freq, None, ALU.mult))
            st.link(V.tensor_scalar(rt2, rt1, 1.0 / TWO_PI, ROUND, ALU.mult, ALU.add))
            st.link(V.tensor_scalar(rt2, rt2, ROUND, None, ALU.subtract))
            for c in (PI_C1, PI_C2, PI_C3):
                st.link(V.scalar_tensor_tensor(rt1, rt2, -c, rt1, ALU.mult, ALU.add))
            st.link(V.tensor_scalar(rt2, rt1, TWO_PI / 4, None, ALU.add))
            st.link(V.tensor_scalar(cosT, rt2, TWO_PI / 2, -TWO_PI, ALU.is_gt, ALU.mult))
            st.link(V.tensor_tensor(rt2, rt2, cosT, ALU.add))
            st.link(V.tensor_scalar(rt1, rt1, PI, -PI, ALU.min, ALU.max))
            V.tensor_scalar(rt2, rt2, PI, -PI, ALU.min, ALU.max).then_inc(angle_ready, 1)

            dve.wait_ge(csil_ready, 1)

            def normalise():
                dve.wait_ge(std_ready, 1)
                st.link(V.reciprocal(rstd[:, 0:TT], std[:, 0:TT]))
                for t in range(TT):
                    V.tensor_scalar(xt[:, t, :], xt[:, t, :], rstd[:, t:t + 1], None, ALU.mult).then_inc(xn_ready, 1)

            for j in range(2):
                if j:
                    dve.wait_ge(modT_done, 1)
                for k in range(KT):
                    dve.wait_ge(ada_in[k % 4], 16 * (KT // 4 * j + k // 4 + 1))
                    if k == 0:
                        ins = V.tensor_scalar(acc, ring_flat[0], csil[:, 0:1], None, ALU.mult)
                    else:
                        ins = V.scalar_tensor_tensor(acc, ring_flat[k % 4], csil[:, k:k + 1], acc, ALU.mult, ALU.add)
                    ins.then_inc(ada_used, 1)
                    dve.wait_ge(ada_used, KT * j + k + 1)
                    if j == 0 and k == 10:
                        normalise()
            dve.wait_ge(modT_done, 1)
            st.link(V.tensor_tensor(colA, ps[:, 6, 0:KT], adab[:, 1, :], ALU.add))
            st.link(V.scalar_tensor_tensor(colA, colA, 1.0, gain[:, 0, :], ALU.add, ALU.mult))
            dve.wait_ge(modT_done, 2)
            V.tensor_tensor(colB, ps[:, 7, 0:KT], adab[:, 0, :], ALU.add).then_inc(ab_ready, 1)

            dve.wait_ge(trig_ready, 2)
            st.link(V.tensor_scalar(sinT, sinT, sgn, None, ALU.mult))
            st.link(V.memset(u[:, :, 0:CW - 1], 0.0))
            for i in range(2):
                for m in range(4):
                    dve.wait_ge(sig_ready, 4 * i + m + 1)
                    dve.wait_ge(proj_done, 8 * i + 4 + m + 1)
                    V.tensor_tensor(u[:, 4 * i + m, CW - 1:], ps[:, m, :], sig[:, m, :], ALU.mult).then_inc(glu_ready, 1)

            def conv_pair(c0):
                last = {}
                for j in range(CW):
                    for c in (c0, c0 + 1):
                        tap = sc_w[:, c, j:j + 1]
                        src = u[:, c, j:j + S]
                        if j == 0:
                            last[c] = st.did(V.tensor_scalar(cv[:, c, :], src, tap, sml[:, S_CB + c:S_CB + c + 1], ALU.mult, ALU.add))
                        else:
                            st.seen(last[c])
                            ins = V.scalar_tensor_tensor(cv[:, c, :], src, tap, cv[:, c, :], ALU.mult, ALU.add)
                            if j < CW - 1:
                                last[c] = st.did(ins)
                            else:
                                ins.then_inc(conv_ready, 1)

            def rope(dst, g, h, bank, n):
                dve.wait_ge(proj_done, n)
                dil = DILATIONS[g]
                src = ps[:, bank, :]
                st.did(V.tensor_tensor(rt1, src, cosT, ALU.mult))
                st.did(V.tensor_tensor(rt2[0:64, :], src[64:128, :], sinT[0:64, :], ALU.mult))
                st.link(V.tensor_tensor(rt2[64:128, :], src[0:64, :], sinT[64:128, :], ALU.mult))
                o = dst[:, h, :]
                if dil == 1:
                    ins = V.tensor_tensor(o, rt1, rt2, ALU.add)
                else:
                    ins = V.tensor_tensor(o.rearrange("p (r l) -> p l r", r=TT), rt1.rearrange("p (l r) -> p l r", r=TT),
                                          rt2.rearrange("p (l r) -> p l r", r=TT), ALU.add)
                ins.then_inc(rope_ready, 1)
                return ins

            dve.wait_ge(glu_ready, 8)
            for g in range(NG):
                W0 = 0 if g == 0 else P
                for part, dst in ((0, q_sb), (1, k_sb)):
                    for h in range(HG):
                        n = 8 * g + 4 * part + h
                        if n:
                            dve.wait_ge(rope_ready, n)
                        rope(dst, g, h, 4 * (1 - part) + h, 16 + 12 * g + 4 * part + h + 1)
                    if g < 2:
                        conv_pair(4 * g + 2 * part)
                for h in range(HG):
                    H = HG * g + h
                    S_ = psum[:, 1024 * (h % 2):1024 * (h % 2) + 1024].rearrange("p (b k) -> p b k", b=TT)
                    dve.wait_ge(s_done, H + 1)
                    if H >= 2:
                        dve.wait_ge(pT_done, H - 1)
                    m_ = mask0 if g == 0 else mask1[g].unsqueeze(1).to_broadcast([P, TT, P])
                    part = sm[h % 2][:, :, W0:]
                    V.scalar_tensor_tensor(part, S_[:, :, W0:], SCALE, m_, ALU.mult, ALU.add).then_inc(s_read, 1)
                    dve.wait_ge(s_read, H + 1)
                    mx = o_sb[:, :, HG * DH + h]
                    if g and h == 0:
                        dve.wait_ge(o_stored, 16 * TT * g)
                    st.link(V.tensor_reduce(mx, part, AX, ALU.max))
                    V.tensor_tensor(part, part, mx.unsqueeze(2).to_broadcast([P, TT, 2 * P - W0]), ALU.subtract).then_inc(centred, 1)
                    dve.wait_ge(p_ready, H + 1)
                    V.tensor_reduce(o_sb[:, :, HG * DH + HG + h], part, AX, ALU.add).then_inc(z_ready, 1)

            dve.wait_ge(lnsum_done, 1)
            for c in range(CO):
                V.scalar_tensor_tensor(cv[:, c, :], ps[:, 7, :], -1.0 / CC, cv[:, c, :], ALU.mult, ALU.add).then_inc(ln_centred, 1)

            dve.wait_ge(stats_in, 16 * NG)
            mx_ = stats[:, :, :, 0:HG]
            zz_ = stats[:, :, :, HG:]
            st.link(V.tensor_tensor(stat_m, mx_[:, :, 0, :], mx_[:, :, 1, :], ALU.max))
            st.link(V.tensor_tensor(stat_m, stat_m, mx_[:, :, 2, :], ALU.max))
            for g in range(NG):
                V.tensor_tensor(coef[:, :, g, :], mx_[:, :, g, :], stat_m, ALU.subtract).then_inc(gap_ready, 1)
            dve.wait_ge(gexp_ready, 1)
            st.link(V.tensor_tensor(zz_, zz_, coef, ALU.mult))
            st.link(V.tensor_tensor(stat_d, zz_[:, :, 0, :], zz_[:, :, 1, :], ALU.add))
            st.link(V.tensor_tensor(stat_d, stat_d, zz_[:, :, 2, :], ALU.add))
            st.link(V.reciprocal(stat_d, stat_d))
            for g in range(NG):
                st.did(V.tensor_tensor(coef[:, :, g, :], coef[:, :, g, :], stat_d, ALU.mult))
            st.seen(st.n)

            dve.wait_ge(lnsq_done, 1)
            V.tensor_scalar(ln_std, ps[:, 7, :], 1.0 / CC, EPS, ALU.mult, ALU.add).then_inc(ln_var, 1)
            dve.wait_ge(ln_std_ready, 1)
            st.link(V.reciprocal(ln_r, ln_std))
            for c in range(CO):
                V.tensor_tensor(cv[:, c, :], cv[:, c, :], ln_r, ALU.mult).then_inc(ln_norm, 1)
            for t in range(TT):
                dve.wait_ge(og_in[t], 16)
                for g in range(NG):
                    for h in range(HG):
                        part = og[t][:, g, h * DH:(h + 1) * DH]
                        dst = og[t][:, 0, h * DH:(h + 1) * DH]
                        cf = coef[:, t, g, h:h + 1]
                        if g == 0:
                            ins = V.tensor_scalar(dst, part, cf, None, ALU.mult)
                        else:
                            dve.wait_ge(og_used, HG * (NG * t + g - 1) + h + 1)
                            ins = V.scalar_tensor_tensor(dst, part, cf, dst, ALU.mult, ALU.add)
                        ins.then_inc(og_used, 1)

            def branch(cg, first):
                if not first:
                    dve.wait_ge(adaT_done, cg)
                for k in range(KT):
                    s = k % 2
                    dve.wait_ge(ada2_in[s], 16 * (KT // 2 * cg + k // 2 + 1))
                    if k == 0:
                        ins = V.tensor_scalar(acc, ada_ring[s], csil[:, 0:1], None, ALU.mult)
                    else:
                        ins = V.scalar_tensor_tensor(acc, ada_ring[s], csil[:, k:k + 1], acc, ALU.mult, ALU.add)
                    ins.then_inc(ada2_used, 1)
                    dve.wait_ge(ada2_used, KT * cg + k + 1)
                for b, sg in ((0, sga), (1, sgc)):
                    for m in range(4):
                        dve.wait_ge(gate_sig, 8 * cg + 4 * b + m + 1)
                        dve.wait_ge(proj_done, 52 + 16 * cg + 8 + 4 * b + m + 1)
                        V.tensor_tensor(sg[:, m, :], sg[:, m, :], ps[:, 4 * b + m, :], ALU.mult).then_inc(branch_done, 1)
                for m in range(4):
                    dve.wait_ge(branch_done, 8 * cg + 4 + m + 1)
                    V.tensor_tensor(mixT[:, bass.ds(4 * cg + m, 1), :], sga[:, m, :], sgc[:, m, :], ALU.add).then_inc(mix_ready, 1)

            branch(0, True)
            with dve.Fori(1, 4) as cg:
                branch(cg, False)

            dve.wait_ge(adaT_read, 4)
            st.link(V.tensor_tensor(modc, modc, adab[:, 2:6, :], ALU.add))
            st.did(V.tensor_tensor(modc[:, 0, :], modc[:, 0, :], gain[:, 1, :], ALU.mult))
            st.did(V.scalar_tensor_tensor(modc[:, 2, :], modc[:, 2, :], 1.0, gain[:, 2, :], ALU.add, ALU.mult))
            V.tensor_tensor(modc[:, 3, :], modc[:, 3, :], gain[:, 3, :], ALU.mult).then_inc(modc_ready, 1)

            dve.wait_ge(rows_in, 48)
            dve.wait_ge(proj_done, 116)
            for t in range(TT):
                dve.wait_ge(ystd_ready, t + 1)
                dve.wait_ge(xb_in[t % 2], 16 * (t // 2 + 1))
                st.link(V.reciprocal(rstd[:, t:t + 1], std[:, t:t + 1]))
                st.link(V.scalar_tensor_tensor(y_sb[:, t, :], y_sb[:, t, :], rstd[:, t:t + 1], rowG1, ALU.mult, ALU.mult))
                V.tensor_tensor(xb[t % 2], xb[t % 2], y_sb[:, t, :], ALU.add).then_inc(x2_ready, 1)
                dve.wait_ge(x2std_ready, t + 1)
                st.link(V.reciprocal(rstd[:, TT + t:TT + t + 1], std[:, TT + t:TT + t + 1]))
                st.link(V.scalar_tensor_tensor(h2[:, t, :], xb[t % 2], rstd[:, TT + t:TT + t + 1], rowA2, ALU.mult, ALU.mult))
                V.tensor_tensor(h2[:, t, :], h2[:, t, :], rowB2, ALU.add).then_inc(h2_ready, 1)

            dve.wait_ge(h2_ready, TT)

            def top16(vals, inds, src, spare, signal=None):
                st.link(V.max(vals[:, 0:8], src))
                st.did(V.max_index(inds[:, 0:8], vals[:, 0:8], src))
                st.link(V.match_replace(spare, vals[:, 0:8], src, LOWEST))
                st.link(V.max(vals[:, 8:16], spare))
                ins = V.max_index(inds[:, 8:16], vals[:, 8:16], spare)
                if signal is None:
                    st.link(ins)
                else:
                    ins.then_inc(signal, 1)

            with dve.Fori(0, 4) as n:
                st.enter(n, ROUTE_STEPS)
                for m in range(4):
                    hold(dve, sc_ready, 4 * n + m + 1, passed_waits)
                    for t in range(TT):
                        top16(v12[:, m, t, :], i12[:, m, t, :], sc[:, m, t, :], s2nd,
                              sc_used if (m, t) == (3, TT - 1) else None)
                hold(dve, sc_used, n + 1, passed_waits)
                st.link(V.tensor_copy(i12f, i12))
                for hh in range(2):
                    for t in range(TT):
                        j = hh * TT + t
                        a_ = v12[:, 2 * hh, t, :].unsqueeze(2).to_broadcast([P, TK, TK])
                        b_ = v12[:, 2 * hh + 1, t, :].unsqueeze(1).to_broadcast([P, TK, TK])
                        st.link(V.tensor_tensor(cand[:, j, :].rearrange("p (a b) -> p a b", a=TK), a_, b_, ALU.add))
                        top16(top[:, j, :], topi[:, j, :], cand[:, j, :], cand2)
                V.tensor_tensor(ex, top, top[:, :, 0:1].to_broadcast([P, CB, TK]), ALU.subtract).then_inc(gap2_ready, 1)
                st.did(V.tensor_scalar(ca, topi, 4, None, ALU.logical_shift_right))
                st.link(V.tensor_scalar(cb, topi, TK - 1, None, ALU.bitwise_and))
                st.did(V.tensor_copy(caf, ca))
                st.link(V.tensor_copy(cbf, cb))
                io = iota.unsqueeze(1).to_broadcast([P, CB * TK, TK])
                for src, half, dst in ((caf, 0, ea), (cbf, 1, eb)):
                    pick = src.rearrange("p c s -> p (c s)").unsqueeze(2).to_broadcast([P, CB * TK, TK])
                    st.link(V.tensor_tensor(hot, pick, io, ALU.is_equal))
                    for hh in range(2):
                        for t in range(TT):
                            j = hh * TT + t
                            hot_j = hot[:, j * TK:(j + 1) * TK, :]
                            st.did(V.tensor_tensor(hot_j, hot_j, i12f[:, 2 * hh + half, t, :].unsqueeze(1).to_broadcast([P, TK, TK]), ALU.mult))
                    st.seen(st.off + st.n)
                    st.link(V.tensor_reduce(dst.rearrange("p c s -> p (c s)"), hot, AX, ALU.add))
                dve.wait_ge(exp2_ready, n + 1)
                st.link(V.tensor_reduce(den, ex, AX, ALU.add))
                st.link(V.reciprocal(rden, den))
                for hh in range(2):
                    js = slice(hh * TT, (hh + 1) * TT)
                    at = idx.rearrange("p (t h s) -> p t h s", t=TT, h=PH)[:, :, bass.ds(2 * n + hh, 1), :]
                    gt = gate.rearrange("p (t h s) -> p t h s", t=TT, h=PH)[:, :, bass.ds(2 * n + hh, 1), :]
                    st.did(V.scalar_tensor_tensor(at, ea[:, js, :].unsqueeze(2), float(P), eb[:, js, :].unsqueeze(2), ALU.mult, ALU.add))
                    ins = (V.tensor_tensor(gt, ex[:, js, :].unsqueeze(2), rden[:, js].unsqueeze(2).unsqueeze(3).to_broadcast([P, TT, 1, TK]), ALU.mult))
                    if hh == 0:
                        st.did(ins)
                ins.then_inc(routed, 1)
                st.leave(4)

            def unit(n, first=False):
                for s in range(TK):
                    dve.wait_ge(d_in[s % NB], 16 * (2 * n + s // NB + 1))
                    row = d_row[s % NB]
                    V.tensor_tensor_reduce(row, row, h2p, 1.0, 0.0, ALU.mult, ALU.add, pre[:, s:s + 1]).then_inc(dots_done, 1)
                dve.wait_ge(gelu_ready, n + 1)
                if not first:
                    dve.wait_ge(diag_ready, TK * n)
                V.tensor_tensor(actv, gel, gate[:, bass.ds(n * TK, TK)], ALU.mult).then_inc(act_ready, 1)

            def finish(t):
                dve.wait_ge(zstd_ready, t + 1)
                dve.wait_ge(x2b_in, 16 * (t + 1))
                st.link(V.reciprocal(zq[:, 2:3], zq[:, 1:2]))
                st.link(V.scalar_tensor_tensor(zs, zs, zq[:, 2:3], rowG3, ALU.mult, ALU.mult))
                V.tensor_tensor(zs, zs, x2b, ALU.add).then_inc(out_ready, 1)

            dve.wait_ge(routed, 4)
            dve.wait_ge(g3_in, 16)
            dve.wait_ge(h2p_ready, 1)
            unit(0, True)
            with dve.Fori(1, PH) as h:
                unit(h)
            with dve.Fori(1, TT) as t:
                st.enter(t - 1, 2)
                hold(dve, h2p_ready, t + 1, passed_waits)
                with dve.Fori(0, 2) as h:
                    unit(PH * t + h)
                finish(t - 1)
                with dve.Fori(2, PH) as h:
                    unit(PH * t + h)
                st.leave(TT - 1)
            finish(TT - 1)


_OUT = ((1, S, D), "float32")


def constants():
    import numpy as np
    c = np.zeros((P, C_END), np.float32)
    c[:, C_ID:C_ID + P] = np.eye(P)
    c[:, C_ONE:C_ONE + P] = 1.0
    q = np.arange(P)[:, None]
    k = np.arange(P)[None, :]
    m0 = np.zeros((P, TT, 2 * P), np.float32)
    m0[:, :, :P] = np.where(k >= q, 0.0, MASK)[:, None, :]
    m0[:, 0, :P] = MASK
    m0[:, :, P:] = np.where(k <= q, 0.0, MASK)[:, None, :]
    c[:, C_M0:C_M0 + TT * 2 * P] = m0.reshape(P, -1)
    c[:, C_M1:C_M1 + P] = np.where(k <= q, 0.0, MASK)
    c[:, C_M2:C_M2 + P] = np.where((k <= q) & (k % 4 == q % 4), 0.0, MASK)
    inv = np.float32(10000.0) ** (-np.arange(0, DH, 2, dtype=np.float32) / np.float32(DH))
    c[:, C_INV] = np.concatenate([inv, inv])
    c[:, C_SGN] = np.where(np.arange(P) < 64, -1.0, 1.0)
    c[:, C_EPS] = EPS
    c[:, C_IOTA:C_IOTA + TK] = np.arange(TK)
    return c


def kernel(x, c, positions, ada_w, ada_b, norm_gains, w_in, w_attn_o, conv_w, conv_b, conv_ln_g, conv_ln_b,
           w_conv_o, w_out, peer_w_q, peer_sub_keys, peer_down, peer_up):
    import numpy as np
    import concourse.bacc as bacc
    from concourse.bass_utils import run_bass_kernel_spmd

    def columns(a, n):
        return np.asarray(a).reshape(n, P).T

    small = np.concatenate([
        columns(c, KT), columns(ada_b, 6 * KT), columns(norm_gains, 4 * KT), columns(conv_b, CO),
        columns(conv_ln_g, CO), columns(conv_ln_b, CO),
        np.asarray(conv_w).reshape(CW, CO, P).transpose(2, 1, 0).reshape(P, CO * CW)], axis=1)
    keysT = np.asarray(peer_sub_keys).reshape(2 * PH, P, P).transpose(2, 0, 1).reshape(P, 2 * PH * P)
    ins = {
        "x": np.asarray(x)[0], "ada_w": np.asarray(ada_w)[0], "w_in": np.asarray(w_in)[0],
        "w_attn_o": np.asarray(w_attn_o)[0], "w_conv_o": np.asarray(w_conv_o)[0], "w_out": np.asarray(w_out)[0],
        "w_q": np.asarray(peer_w_q)[0], "down": np.asarray(peer_down)[0], "up": np.asarray(peer_up)[0],
        "keysT": keysT, "pos": np.asarray(positions), "small": small, "const": constants(),
    }
    nc = bacc.Bacc("TRN2", target_bir_lowering=False, num_devices=1)
    arrays, args = {}, []
    for name, a in ins.items():
        arrays[f"in_{name}"] = np.ascontiguousarray(a)
        args.append(nc.dram_tensor(f"in_{name}", a.shape, mybir.dt.from_np(a.dtype), kind="ExternalInput").ap())
    out = nc.dram_tensor("out_0", (S, D), mybir.dt.float32, kind="ExternalOutput").ap()
    block_kernel(nc, *args, out)
    r = run_bass_kernel_spmd(nc, [arrays], core_ids=[0])
    return r.results[0]["out_0"].reshape(1, S, D)
```

```python
import concourse.bass as bass
from concourse import mybir
from contextlib import ExitStack

D = 2048
S = 512
P = 128
DH = 128
HG = 4
NG = 3
DILATIONS = (1, 4, 16)
AW = NG * HG * DH
CC = D // 2
CW = 31
CO = CC // P
PH = 8
TK = 16
KT = D // P
TT = S // P
NT = 512
EPS = 1e-6
SCALE = float(DH) ** -0.5
MASK = -1e30
LOWEST = -3.4028235e38
GLU0 = 3 * AW
GATE0 = GLU0 + 2 * CC
UNITS = TT * PH
U_GATES = 3 * (4 + 3 * NG)
U_OUT = U_GATES + 4 * 8
U_Q = U_OUT + 4 * 3
FRONT = 112


def mix_at(k):
    return 12 - 4 * (k // 4) + k % 4


TILE_STEPS = 165
NB = 8
UB = 4


C_ID = 0
C_ONE = C_ID + P
C_INV = C_ONE + P
C_SGN = C_INV + 1
C_EPS = C_SGN + 1
C_IOTA = C_EPS + 1
C_M0 = C_IOTA + TK
C_M1 = C_M0 + TT * 2 * P
C_M2 = C_M1 + P
C_END = C_M2 + P

S_C = 0
S_ADAB = S_C + KT
S_GAIN = S_ADAB + 6 * KT
S_CB = S_GAIN + 4 * KT
S_LG = S_CB + CO
S_LB = S_LG + CO
S_CW = S_LB + CO
S_END = S_CW + CO * CW

TWO_PI = 6.283185307179586
PI = 3.1415925
PI_C1 = 6.28125
PI_C2 = 0.0019350051879882812
PI_C3 = TWO_PI - PI_C1 - PI_C2
ROUND = 12582912.0


def hold(eng, sem, value, passed):
    eng.wait_ge(sem, value)
    if not isinstance(value, int):
        eng.sem_inc(passed, 1)


class Steps:

    def __init__(self, eng, sem, passed):
        self.eng, self.sem, self.n, self.off, self.stack = eng, sem, 0, 0, []
        self.passed = passed

    def did(self, ins):
        ins.then_inc(self.sem, 1)
        self.n += 1
        return self.off + self.n

    def seen(self, value):
        hold(self.eng, self.sem, value, self.passed)

    def link(self, ins):
        self.seen(self.did(ins))

    def enter(self, i, per):
        self.stack.append((self.n, self.off, per))
        self.off = self.off + i * per

    def leave(self, count):
        n, off, per = self.stack.pop()
        assert self.n - n == per, (self.n - n, per)
        self.n, self.off = n + per * count, off


def block_kernel(nc, x, ada_w, w_in, w_attn_o, w_conv_o, w_out, w_q, down, up, keysT, pos, small, const, out):
    fp32 = mybir.dt.float32
    fp32r = mybir.dt.float32r
    i32 = mybir.dt.int32
    u32 = mybir.dt.uint32
    ALU = mybir.AluOpType
    ACT = mybir.ActivationFunctionType
    AX = mybir.AxisListType.X

    ctx = ExitStack()
    with ctx:
        def sem(name):
            return ctx.enter_context(nc.semaphore(name))

        front = ctx.enter_context(nc.sbuf_tensor("front", [P, FRONT * 256], fp32))
        front_start = nc.sbuf_base - FRONT * 1024
        back = ctx.enter_context(nc.sbuf_tensor("back", [P, 24528], fp32))
        psum = ctx.enter_context(nc.psum_tensor("psum", [P, 8 * 512], fp32))
        ps = psum[:, :].rearrange("p (b n) -> p b n", b=8)
        KB = 256

        def view(kb, *dims):
            size = 1
            for d in dims:
                size *= d
            where, start = (front, int(kb * KB)) if kb < FRONT else (back, int(kb * KB) - FRONT * KB)
            a = where[:, start:start + size]
            if len(dims) == 2:
                return a.rearrange("p (a b) -> p a b", a=dims[0])
            if len(dims) == 3:
                return a.rearrange("p (a b c) -> p a b c", a=dims[0], b=dims[1])
            return a

        def parts(name, kb, a, b):
            t = nc.alloc_sbuf_tensor_at(name, [P, a * b], fp32r, offset=front_start + kb * 1024)
            return t[:, :].rearrange("p (a b) -> p a b", a=a)

        w_low = parts("w_low", 0, 16, NT)
        x_high = parts("x_high", 32, KT, S)
        x_low = parts("x_low", 64, KT, S)
        w_high = parts("w_high", 96, 8, NT)
        wl = [w_low[:, 4 * s:4 * s + 4, :] for s in range(4)]
        wh = [w_high[:, 4 * s:4 * s + 4, :] for s in range(2)]

        ring = [view(8 * s, 4, NT) for s in range(4)]
        ring_flat = [view(8 * s, D) for s in range(4)]
        junk0 = view(32, D)
        xt = view(112, TT, D)
        mixT = view(112, KT, S)
        sig = view(112, HG, S)
        sm = [view(112 + 4 * b, TT, 2 * P) for b in range(2)]
        probT = [view(120 + 4 * b, TT * 2, P) for b in range(2)]
        o_sb = view(128, TT, HG * DH + 2 * HG)
        OW = HG * DH + 2 * HG
        og = [view(112 + 6 * t, NG, HG * DH) for t in range(TT)]
        UW = S + CW - 1
        u = view(144, CO, UW)
        cv = u[:, :, 0:S]
        cosT = view(161, S)
        sinT = view(163, S)
        rt1 = view(165, S)
        rt2 = view(167, S)
        ln_std = view(165, S)
        ln_r = view(167, S)
        attnT = view(161, HG, S)
        q_sb = view(169, HG, S)
        k_sb = view(177, HG, S)
        v_sb = view(185, TT, HG * DH)
        sgc = view(169, HG, S)
        sq = view(177, CO, S)
        acc = view(177, D)
        ada_ring = [view(185 + 4 * s, D // 2) for s in range(2)]
        cst = view(193, C_END)
        sml = view(199.25, S_END)
        csil = view(201, KT)
        colA = view(201.1, KT)
        colB = view(201.2, KT)
        modc = view(201.3, 4, KT)
        modc_flat = view(201.3, 4 * KT)
        modr = view(201.6, P)
        ssq = view(202.2, 2 * TT)
        std = view(202.3, 2 * TT)
        rstd = view(202.4, 2 * TT)
        ssqy = view(202.5, TT, 4)
        h_tmp = [view(203.5 + 2 * b, S) for b in range(2)]
        conv_sum = [view(203.5 + 2 * b, S) for b in range(2)]
        stats = view(203.5, TT, NG, 2 * HG)
        coef = view(204, TT, NG, HG)
        stat_m = view(204.3, TT, HG)
        stat_d = view(204.5, TT, HG)
        ident = cst[:, C_ID:C_ID + P]
        ones = cst[:, C_ONE:C_ONE + P]
        mask0 = cst[:, C_M0:C_M0 + TT * 2 * P].rearrange("p (b k) -> p b k", b=TT)
        mask1 = [None, cst[:, C_M1:C_M1 + P], cst[:, C_M2:C_M2 + P]]
        inv_freq = cst[:, C_INV:C_INV + 1]
        sgn = cst[:, C_SGN:C_SGN + 1]
        eps = cst[:, C_EPS:C_EPS + 1]
        iota = cst[:, C_IOTA:C_IOTA + TK]
        sc_w = sml[:, S_CW:S_CW + CO * CW].rearrange("p (c j) -> p c j", c=CO)
        gain = sml[:, S_GAIN:S_GAIN + 4 * KT].rearrange("p (g k) -> p g k", g=4)
        adab = sml[:, S_ADAB:S_ADAB + 6 * KT].rearrange("p (g k) -> p g k", g=6)
        rowG1, rowA2, rowB2, rowG3 = (view(112 + 8 * j, D) for j in range(4))
        y_sb = view(144, TT, D)
        h2 = view(144, TT, D)
        xb = [view(176 + 8 * b, D) for b in range(2)]
        keys = view(112, KT, P)
        qs = view(120, HG, S)
        sc = [view(kb, HG, TT, P) for kb in (128, 176, 184, 104)]
        cand = view(194.1, 2, TK * TK)
        hot = view(194.1, 4 * TK, TK)
        sc_part = view(198.1, HG, P)
        v12 = view(200.1, HG, TK)
        i12 = view(200.4, HG, TK).bitcast(u32)
        i12f = view(200.7, HG, TK)
        top = view(201, 2, TK)
        topi = view(201.2, 2, TK).bitcast(u32)
        pair = view(201.4, 2, 2, TK).bitcast(u32)
        pairf = view(201.7, 2 * 2 * TK)
        picked = view(202, 2, 2, TK)
        den = view(202.3, PH)
        rden = view(202.4, PH)
        idx = view(203.5, UNITS * TK).bitcast(u32)
        gate = view(205.5, UNITS * TK)
        d_row = [view(8 * s, D) for s in range(NB)]
        u_row = [view(64 + 8 * s, D) for s in range(UB)]
        zs = view(96, D)
        x2b = view(120, D)
        diag = view(112, TK, P)
        pre = view(192, TK)
        gel = view(192.1, TK)
        actv = view(192.2, TK)
        stage = [view(192.3 + 0.1 * s, TK).bitcast(u32) for s in range(3)]
        zq = view(192.6, 4)
        h2p = psum[:, 0:D]
        zacc = psum[:, D:2 * D]

        scr_o = nc.dram_tensor("attn_parts", [NG, S, OW], fp32, kind="Internal").ap()
        scr_m = nc.dram_tensor("mod_rows", [4, D], fp32, kind="Internal").ap()
        scr_x = nc.dram_tensor("x_after_mixing", [TT, P, D], fp32, kind="Internal").ap()

        consts_in = sem("consts_in")
        passed_waits = sem("passed_waits")
        pos_in = sem("pos_in")
        x_in = [sem(f"x_in{t}") for t in range(TT)]
        ada_in = [sem(f"ada_in{s}") for s in range(4)]
        ada_used = sem("ada_used")
        ada2_in = [sem(f"ada2_in{s}") for s in range(2)]
        ada2_used = sem("ada2_used")
        w_in_sem = [sem(f"w_in{s}") for s in range(4)]
        w_used = sem("w_used")
        w_high_done, w_low_done = sem("w_high_done"), sem("w_low_done")
        h_high = sem("h_high")
        mix_high, mix_split = sem("mix_high"), sem("mix_split")
        h2_high = sem("h2_high")
        ysum_ready = sem("ysum_ready")
        csil_ready = sem("csil_ready")
        xn_ready = sem("xn_ready")
        std_ready = sem("std_ready")
        xT_done = sem("xT_done")
        modT_done = sem("modT_done")
        ab_ready = sem("ab_ready")
        hT_ready = sem("hT_ready")
        angle_ready = sem("angle_ready")
        trig_ready = sem("trig_ready")
        proj_done = sem("proj_done")
        sig_ready = sem("sig_ready")
        glu_ready = sem("glu_ready")
        rope_ready = sem("rope_ready")
        v_ready = sem("v_ready")
        s_done = sem("s_done")
        s_read = sem("s_read")
        centred = sem("centred")
        p_ready = sem("p_ready")
        z_ready = sem("z_ready")
        pT_done = sem("pT_done")
        pT_ready = sem("pT_ready")
        pv_done = sem("pv_done")
        o_ready = sem("o_ready")
        o_stored = sem("o_stored")
        stats_in = sem("stats_in")
        og_in = [sem(f"og_in{t}") for t in range(TT)]
        og_used = sem("og_used")
        gap_ready = sem("gap_ready")
        gexp_ready = sem("gexp_ready")
        attnT_done = sem("attnT_done")
        attnT_ready = sem("attnT_ready")
        conv_ready = sem("conv_ready")
        lnsum_done = sem("lnsum_done")
        ln_centred = sem("ln_centred")
        ln_sq = sem("ln_sq")
        lnsq_done = sem("lnsq_done")
        ln_var = sem("ln_var")
        ln_std_ready = sem("ln_std_ready")
        ln_norm = sem("ln_norm")
        convT_ready = sem("convT_ready")
        gate_sig = sem("gate_sig")
        branch_done = sem("branch_done")
        mix_ready = sem("mix_ready")
        adaT_done = sem("adaT_done")
        adaT_read = sem("adaT_read")
        modc_ready = sem("modc_ready")
        modr_done = sem("modr_done")
        modr_ready = sem("modr_ready")
        modr_stored = sem("modr_stored")
        rows_in = sem("rows_in")
        g3_in = sem("g3_in")
        y_ready = sem("y_ready")
        xb_in = [sem(f"xb_in{b}") for b in range(2)]
        ystd_ready = sem("ystd_ready")
        x2_ready = sem("x2_ready")
        x2_stored = [sem(f"x2_stored{b}") for b in range(2)]
        x2std_ready = sem("x2std_ready")
        h2_ready = sem("h2_ready")
        h2T_done = sem("h2T_done")
        h2T_ready = sem("h2T_ready")
        keys_in = sem("keys_in")
        q_ready = sem("q_ready")
        sc_done = sem("sc_done")
        sc_ready = sem("sc_ready")
        gap2_ready = sem("gap2_ready")
        exp2_ready = sem("exp2_ready")
        routed = sem("routed")
        d_in = [sem(f"d_in{s}") for s in range(NB)]
        u_in = [sem(f"u_in{s}") for s in range(UB)]
        staged = sem("staged")
        dots_done = sem("dots_done")
        u_used = sem("u_used")
        h2p_ready = sem("h2p_ready")
        gelu_ready = sem("gelu_ready")
        act_ready = sem("act_ready")
        diag_ready = sem("diag_ready")
        z_read = sem("z_read")
        zstd_ready = sem("zstd_ready")
        x2b_in = sem("x2b_in")
        out_ready = sem("out_ready")
        out_stored = sem("out_stored")
        dve_step, act_step = sem("dve_step"), sem("act_step")

        block = ctx.enter_context(nc.Block())

        @block.sync
        def _(sp):
            def ada_load(j, k, s):
                nc.sync.dma_start(ring_flat[s], ada_w[bass.ds(k * P, P), j * D:(j + 1) * D]).then_inc(ada_in[s], 16)

            for s in range(4):
                ada_load(1, s, s)
            with sp.Fori(1, 4) as i:
                for s in range(4):
                    sp.wait_ge(ada_used, 4 * (i - 1) + s + 1)
                    ada_load(1, 4 * i + s, s)
            with sp.Fori(0, 4) as i:
                for s in range(4):
                    sp.wait_ge(ada_used, 4 * (i + 3) + s + 1)
                    ada_load(0, 4 * i + s, s)

            def chunk(s, w, row0, rows, c0):
                nc.sync.dma_start(ring[s][:, 0:rows // P, :], w[row0:row0 + rows, bass.ds(c0, NT)]
                                  .rearrange("(k p) c -> p k c", p=P)).then_inc(w_in_sem[s], 16)

            def w_load(w, c0, used, before):
                for s in range(4):
                    if s < 3:
                        hold(sp, w_used, used - 3 + s + 1, passed_waits)
                    else:
                        hold(sp, proj_done, before, passed_waits)
                    chunk(s, w, s * NT, NT, c0)

            for s in range(4):
                sp.wait_ge(ada_used, 2 * KT - 3 + s)
                chunk(s, w_in, s * NT, NT, GLU0 + CC)
            w_load(w_in, GLU0, 3, 4)
            w_load(w_in, GLU0 + CC + NT, 6, 8)
            w_load(w_in, GLU0 + NT, 9, 12)
            with sp.Fori(0, NG) as g:
                for part in range(3):
                    w_load(w_in, g * NT + part * AW, 12 + 9 * g + 3 * part, 4 * (4 + 3 * g + part))

            def ada2_load(cg, j0, count):
                for j in range(j0, j0 + count):
                    if not (isinstance(cg, int) and cg == 0 and j < 2):
                        hold(sp, ada2_used, 2 * KT * cg + j - 1, passed_waits)
                    nc.sync.dma_start(ada_ring[j % 2], ada_w[(j // 2) * P:(j // 2 + 1) * P,
                                      bass.ds((2 + cg) * D + (j % 2) * (D // 2), D // 2)]).then_inc(ada2_in[j % 2], 16)

            def slot_free(cg, s):
                if s % 2 == 0:
                    hold(sp, w_used, U_GATES + 8 * cg - 1 + s // 2, passed_waits)
                else:
                    hold(sp, proj_done, 48 + 16 * cg + (4 if s == 3 else 0), passed_waits)

            def branch_load(cg, first):
                per = [0] * 7 + [8] * 4 + [0] if first else [3] * 8 + [2] * 4
                at = 0
                for i in range(12):
                    s = i % 4
                    if i < 4:
                        if not first:
                            slot_free(cg, s)
                        elif s < 3:
                            sp.wait_ge(w_used, U_GATES - 3 + s + 1)
                        else:
                            sp.wait_ge(proj_done, 52)
                        chunk(s, w_in, s * NT, NT, GATE0 + cg * NT)
                    else:
                        if s < 3:
                            hold(sp, w_used, U_GATES + 8 * cg + 3 * (i // 4 - 1) + s + 1, passed_waits)
                        else:
                            hold(sp, proj_done, 52 + 16 * cg + 4 * (i // 4), passed_waits)
                        if i < 8:
                            chunk(s, w_in, s * NT, NT, GATE0 + D + cg * NT)
                        elif s < 2:
                            chunk(s, w_attn_o, s * 2 * P, 2 * P, cg * NT)
                        else:
                            chunk(s, w_conv_o, (s - 2) * NT, NT, cg * NT)
                    if first and at == 0 and per[i]:
                        sp.wait_ge(lnsq_done, 1)
                    ada2_load(cg, at, per[i])
                    at += per[i]

            branch_load(0, True)
            with sp.Fori(1, 4) as cg:
                branch_load(cg, False)
            for s in range(4):
                slot_free(4, s)
                chunk(s, w_out, s * NT, NT, 0)
            with sp.Fori(1, 4) as n:
                w_load(w_out, n * NT, U_OUT + 3 * n, 116 + 4 * n)
            with sp.Fori(0, 4) as n:
                w_load(w_q, n * NT, U_Q + 3 * n, 132 + 4 * n)

            for t in range(TT):
                if t == 0:
                    sp.wait_ge(sc_done, KT)
                else:
                    sp.wait_ge(out_stored, 16 * t)
                sp.wait_ge(x2_stored[t % 2], 16 * (t // 2 + 1))
                nc.sync.dma_start(x2b, scr_x[t, :, :]).then_inc(x2b_in, 16)
                sp.wait_ge(out_ready, t + 1)
                nc.sync.dma_start(out[t * P:(t + 1) * P, :], zs).then_inc(out_stored, 16)
            sp.wait_ge(out_stored, 16 * TT)

        @block.gpsimd
        def _(pool):
            def low(G, s):
                hold(pool, w_high_done, 4 * G + s + 1, passed_waits)
                nc.gpsimd.tensor_tensor(wl[s], ring[s], wh[s % 2].bitcast(fp32), ALU.subtract).then_inc(w_low_done, 1)

            def mix_low(k):
                pool.wait_ge(mix_high, k + 1)
                nc.gpsimd.tensor_tensor(x_low[:, k, :], mixT[:, mix_at(k), :], x_high[:, k, :].bitcast(fp32),
                                        ALU.subtract).then_inc(mix_split, 1)

            with pool.Fori(0, 21) as G:
                for s in range(4):
                    low(G, s)
            for k in range(12):
                mix_low(k)
            low(21, 0)
            low(21, 1)
            for k in range(12, KT):
                mix_low(k)
            low(21, 2)
            low(21, 3)
            with pool.Fori(22, 29) as G:
                for s in range(4):
                    low(G, s)

            def gather(table, rows, n, s, into):
                nc.gpsimd.indirect_dma_start(
                    out=rows, out_offset=None, in_=table[:, :],
                    in_offset=bass.IndirectOffsetOnAxis(ap=stage[n][:, s:s + 1], axis=0),
                ).then_inc(into, 16)

            def put_stage(n, b, first=False):
                if not first:
                    hold(pool, u_used, TK * (n - 2) + 1, passed_waits)
                hold(pool, routed, n + 1, passed_waits)
                nc.gpsimd.tensor_copy(stage[b], idx[:, bass.ds(n * TK, TK)]).then_inc(staged, 1)
                hold(pool, staged, n + 1, passed_waits)

            def down_row(n, b, s, first=False):
                if not (first and s < NB):
                    hold(pool, dots_done, TK * n + s - NB + 1, passed_waits)
                gather(down, d_row[s % NB], b, s, d_in[s % NB])

            def up_row(n, b, s, first=False):
                if not (first and s < UB):
                    hold(pool, u_used, TK * n + s - UB + 1, passed_waits)
                gather(up, u_row[s % UB], b, s, u_in[s % UB])

            for b in range(2):
                pool.wait_ge(x2_stored[b], 32)
            pool.wait_ge(q_ready, KT)
            pool.wait_ge(sc_done, KT)
            put_stage(0, 0, first=True)
            for s in range(TK):
                down_row(0, 0, s, first=True)
            put_stage(1, 1, first=True)
            for s in range(TK):
                down_row(1, 1, s)
                up_row(0, 0, s, first=True)
            with pool.Fori(0, 10) as j:
                for p in range(3):
                    i = 3 * j + (p + 1)
                    put_stage(i + 1, (p + 2) % 3)
                    for s in range(TK):
                        down_row(i + 1, (p + 2) % 3, s)
                        up_row(i, (p + 1) % 3, s)
            for s in range(TK):
                up_row(UNITS - 1, (UNITS - 1) % 3, s)

        @block.tensor
        def _(pe):
            def mm(o, a, b, start, stop):
                return nc.tensor.matmul(o, a, b, start=start, stop=stop)

            pe.wait_ge(consts_in, 32)
            def transpose_x(k):
                for t in range(TT):
                    ins = nc.tensor.transpose(ps[:, k % 6, t * P:(t + 1) * P], xt[:, t, k * P:(k + 1) * P], ident)
                ins.then_inc(xT_done, 1)

            def mod_columns(bank):
                for k in range(KT):
                    ins = mm(ps[:, bank, k:k + 1], acc[:, k * P:(k + 1) * P], ones[:, 0:1], True, True)
                return ins

            pe.wait_ge(xn_ready, TT)
            for k in range(6):
                transpose_x(k)
            for j in range(2):
                pe.wait_ge(ada_used, KT * (j + 1))
                mod_columns(6 + j).then_inc(modT_done, 1)
            for k in range(6, KT):
                pe.wait_ge(h_high, k - 5)
                transpose_x(k)

            def product(o, a_high, a_low, b_high, b_low, start, stop):
                mm(o, a_high, b_high, start, False)
                mm(o, a_high, b_low, False, False)
                return mm(o, a_low, b_high, False, stop)

            def project(G, half):
                for s in range(4):
                    pe.wait_ge(w_low_done, 4 * G + s + 1)
                    if isinstance(G, int) and G == 0:
                        pe.wait_ge(hT_ready, max(12, 4 * s + 4))
                    for m in range(4):
                        cols = slice(m * P, (m + 1) * P)
                        for k in range(4):
                            ins = product(ps[:, 4 * half + m, :], wh[s % 2][:, k, cols], wl[s][:, k, cols],
                                          x_high[:, 4 * s + k, :], x_low[:, 4 * s + k, :],
                                          s == 0 and k == 0, s == 3 and k == 3)
                        if s == 3:
                            ins.then_inc(proj_done, 1)
                    if s < 3:
                        ins.then_inc(w_used, 1)

            def project_tokens(G, half, tokens):
                for s in range(4):
                    pe.wait_ge(w_low_done, 4 * G + s + 1)
                    for t in range(TT):
                        for k in range(4):
                            ins = product(ps[:, 4 * half + t, :], tokens(x_high, 4 * s + k, t), tokens(x_low, 4 * s + k, t),
                                          wh[s % 2][:, k, :], wl[s][:, k, :],
                                          s == 0 and k == 0, s == 3 and k == 3)
                        if s == 3:
                            ins.then_inc(proj_done, 1)
                    if s < 3:
                        ins.then_inc(w_used, 1)

            for i in range(2):
                if i:
                    pe.wait_ge(sig_ready, 4)
                project(2 * i, 1)
                if i:
                    pe.wait_ge(glu_ready, 4)
                project(2 * i + 1, 0)

            for g, dil in enumerate(DILATIONS):
                if g == 0:
                    pe.wait_ge(sig_ready, 8)
                project(4 + 3 * g, 1)
                if g == 0:
                    pe.wait_ge(glu_ready, 8)
                project(5 + 3 * g, 0)
                pe.wait_ge(rope_ready, 8 * g + 4)

                def tokens(x_, k, t):
                    if dil == 1:
                        return x_[:, k, t * P:(t + 1) * P]
                    return x_[:, k, :].rearrange("p (l r) -> p r l", r=TT)[:, t, :]

                project_tokens(6 + 3 * g, 1, tokens)
                pe.wait_ge(rope_ready, 8 * g + 8)

                def scores(h):
                    H = HG * g + h
                    if h >= 2:
                        pe.wait_ge(s_read, H - 1)
                    S_ = psum[:, 1024 * (h % 2):1024 * (h % 2) + 1024].rearrange("p (b k) -> p b k", b=TT)
                    for b in range(TT):
                        qb = q_sb[:, h, b * P:(b + 1) * P]
                        if g == 0:
                            pb = max(b - 1, 0)
                            mm(S_[:, b, 0:P], qb, k_sb[:, h, pb * P:(pb + 1) * P], True, True)
                        ins = mm(S_[:, b, P:2 * P], qb, k_sb[:, h, b * P:(b + 1) * P], True, True)
                    ins.then_inc(s_done, 1)

                def turn(h):
                    H = HG * g + h
                    pe.wait_ge(p_ready, H + 1)
                    if h == 0:
                        pe.wait_ge(v_ready, TT * (g + 1))
                    else:
                        pe.wait_ge(pT_ready, H)
                    T_ = psum[:, 2048:3072].rearrange("p (b k) -> p b k", b=8)
                    for b in range(TT):
                        for half in ((0, 1) if g == 0 and b else (1,)):
                            ins = nc.tensor.transpose(T_[:, 2 * b + half, :], sm[h % 2][:, b, half * P:(half + 1) * P], ident)
                    ins.then_inc(pT_done, 1)

                def values(h):
                    H = HG * g + h
                    pe.wait_ge(pT_ready, H + 1)
                    if h >= 2:
                        pe.wait_ge(o_ready, H - 1)
                    for b in range(TT):
                        prev = g == 0 and b > 0
                        o = ps[:, 6 + h % 2, b * DH:(b + 1) * DH]
                        if prev:
                            mm(o, probT[h % 2][:, 2 * b, :], v_sb[:, b - 1, h * DH:(h + 1) * DH], True, False)
                        ins = mm(o, probT[h % 2][:, 2 * b + 1, :], v_sb[:, b, h * DH:(h + 1) * DH], not prev, True)
                    ins.then_inc(pv_done, 1)

                scores(0)
                scores(1)
                for h in range(HG):
                    turn(h)
                    values(h)
                    if h + 2 < HG:
                        scores(h + 2)
                pe.wait_ge(o_ready, HG * (g + 1))
                pe.wait_ge(s_read, HG * (g + 1))

            pe.wait_ge(conv_ready, CO)
            for c in range(CO):
                ins = mm(ps[:, 7, :], ones, cv[:, c, :], c == 0, c == CO - 1)
            ins.then_inc(lnsum_done, 1)

            def branches(cg, first):
                if not first:
                    pe.wait_ge(branch_done, 8 * cg)
                project(13 + 2 * cg, 0)
                if first:
                    pe.wait_ge(ln_centred, CO)
                    for c in range(CO):
                        pe.wait_ge(ln_sq, c + 1)
                        ins = mm(ps[:, 7, :], ones, sq[:, c, :], c == 0, c == CO - 1)
                    ins.then_inc(lnsq_done, 1)
                    pe.wait_ge(ln_var, 1)
                project(14 + 2 * cg, 1)
                pe.wait_ge(gate_sig, 8 * cg + 4)
                if first:
                    for t in range(TT):
                        pe.wait_ge(og_used, HG * NG * (t + 1))
                        for h in range(HG):
                            ins = nc.tensor.transpose(ps[:, t, h * P:(h + 1) * P], og[t][:, 0, h * P:(h + 1) * P], ident)
                        ins.then_inc(attnT_done, 1)
                    pe.wait_ge(attnT_ready, TT)
                for s in range(2):
                    pe.wait_ge(w_in_sem[s], 16 * (16 + 3 * cg))
                    for m in range(4):
                        for k in range(2):
                            ins = mm(ps[:, m, :], ring[s][:, k, m * P:(m + 1) * P], attnT[:, 2 * s + k, :],
                                     s == 0 and k == 0, s == 1 and k == 1)
                        if s == 1:
                            ins.then_inc(proj_done, 1)
                    if s == 0:
                        ins.then_inc(w_used, 1)
                pe.wait_ge(gate_sig, 8 * cg + 8)
                pe.wait_ge(ada2_used, 2 * KT * (cg + 1))
                mod_columns(4).then_inc(adaT_done, 1)
                pe.wait_ge(adaT_read, cg + 1)
                if first:
                    pe.wait_ge(convT_ready, CO)
                for s in range(2):
                    pe.wait_ge(w_in_sem[2 + s], 16 * (16 + 3 * cg))
                    for m in range(4):
                        for k in range(4):
                            ins = mm(ps[:, 4 + m, :], ring[2 + s][:, k, m * P:(m + 1) * P], cv[:, 4 * s + k, :],
                                     s == 0 and k == 0, s == 1 and k == 3)
                        if s == 1:
                            ins.then_inc(proj_done, 1)
                    if s == 0:
                        ins.then_inc(w_used, 1)

            branches(0, True)
            with pe.Fori(1, 4) as cg:
                branches(cg, False)

            pe.wait_ge(branch_done, 32)
            pe.wait_ge(modc_ready, 1)
            nc.tensor.transpose(ps[0:4 * KT, 0, 0:P], modc_flat, ident).then_inc(modr_done, 1)
            pe.wait_ge(modr_ready, 1)

            def mixed(x_, k, t):
                return x_[:, k, t * P:(t + 1) * P]

            pe.wait_ge(mix_split, KT)
            project_tokens(21, 0, mixed)
            project_tokens(22, 1, mixed)
            for half in range(2):
                pe.wait_ge(y_ready, 4 * half + 4)
                project_tokens(23 + half, half, mixed)

            for t in range(TT):
                pe.wait_ge(h2_ready, t + 1)
                if t == 0:
                    pe.wait_ge(y_ready, 16)
                for k4 in range(4):
                    if t >= 2:
                        pe.wait_ge(h2T_ready, 4 * (t - 2) + k4 + 1)
                    for k in range(4):
                        ins = nc.tensor.transpose(ps[:, 4 * (t % 2) + k4, k * P:(k + 1) * P],
                                                  h2[:, t, (4 * k4 + k) * P:(4 * k4 + k + 1) * P], ident)
                    ins.then_inc(h2T_done, 1)

            pe.wait_ge(h2T_ready, 4 * TT)
            pe.wait_ge(keys_in, 16)
            def route_products(n, first=False):
                project(25 + n, 0)
                for m in range(4):
                    pe.wait_ge(q_ready, 4 * n + m + 1)
                    if not first:
                        pe.wait_ge(sc_ready, 4 * n)
                    for t in range(TT):
                        ins = mm(ps[:, 4 + m, t * P:(t + 1) * P], qs[:, m, t * P:(t + 1) * P],
                                 keys[:, bass.ds(4 * n + m, 1), :], True, True)
                    ins.then_inc(sc_done, 1)

            route_products(0, True)
            with pe.Fori(1, 4) as n:
                route_products(n)

            def unit(n, first, last):
                for s in range(TK):
                    pe.wait_ge(diag_ready, TK * n + s + 1)
                    pe.wait_ge(u_in[s % UB], 16 * (4 * n + s // UB + 1))
                    for c in range(4):
                        ins = mm(zacc[:, c * 512:(c + 1) * 512], diag[:, s, :], u_row[s % UB][:, c * 512:(c + 1) * 512],
                                 first and s == 0, last and s == TK - 1)
                    ins.then_inc(u_used, 1)

            pe.wait_ge(sc_ready, KT)

            def tile(t):
                unit(PH * t, True, False)
                with pe.Fori(1, PH - 1) as h:
                    unit(PH * t + h, False, False)
                unit(PH * t + (PH - 1), False, True)

            tile(0)
            with pe.Fori(1, TT) as t:
                pe.wait_ge(z_read, t)
                tile(t)

        @block.scalar
        def _(act):
            st = Steps(act, act_step, passed_waits)
            A = nc.scalar.activation
            nc.scalar.dma_start(sml, small).then_inc(consts_in, 16)
            nc.scalar.dma_start(cst, const).then_inc(consts_in, 16)
            nc.scalar.dma_start(cosT.bitcast(i32), pos[0:1, :].to_broadcast([P, S])).then_inc(pos_in, 16)
            for t in range(TT):
                nc.scalar.dma_start(xt[:, t, :], x[t * P:(t + 1) * P, :]).then_inc(x_in[t], 16)
            act.wait_ge(consts_in, 32)
            A(csil, sml[:, S_C:S_C + KT], ACT.Silu).then_inc(csil_ready, 1)
            for t in range(TT):
                act.wait_ge(x_in[t], 16)
                st.link(A(junk0, xt[:, t, :], ACT.Square, accum_out=ssq[:, t:t + 1]))
            A(std[:, 0:TT], ssq[:, 0:TT], ACT.Sqrt, scale=1.0 / D, bias=eps).then_inc(std_ready, 1)
            act.wait_ge(angle_ready, 1)
            A(sinT, rt1, ACT.Sin).then_inc(trig_ready, 1)
            A(cosT, rt2, ACT.Sin).then_inc(trig_ready, 1)

            def first_high(G, s):
                act.wait_ge(w_in_sem[s], 16 * (G + 1))
                if G or s > 1:
                    if s == 1:
                        act.wait_ge(proj_done, 4 * G)
                    else:
                        act.wait_ge(w_used, 3 * G + (0, 0, 1, 2)[s])
                A(wh[s % 2], ring[s], ACT.Copy).then_inc(w_high_done, 1)

            def later_high(s, rnd, last_used, used, before):
                act.wait_ge(w_in_sem[s], 16 * (rnd + 1))
                if s == 0:
                    act.wait_ge(w_used, last_used)
                elif s == 1:
                    act.wait_ge(proj_done, before)
                else:
                    act.wait_ge(w_used, used + s - 1)
                A(wh[s % 2], ring[s], ACT.Copy).then_inc(w_high_done, 1)

            act.wait_ge(ab_ready, 1)
            for k in range(KT):
                if k == 2:
                    first_high(0, 0)
                if k == 8:
                    first_high(0, 1)
                act.wait_ge(xT_done, k + 1)
                if k >= 2:
                    act.wait_ge(hT_ready, k - 1)
                st.link(A(h_tmp[k % 2], ps[:, k % 6, :], ACT.Identity, scale=colA[:, k:k + 1], bias=colB[:, k:k + 1]))
                A(x_high[:, k, :], h_tmp[k % 2], ACT.Copy).then_inc(h_high, 1)

            first_high(0, 2)
            first_high(0, 3)
            for i in range(2):
                first_high(2 * i + 1, 0)
                for m in range(4):
                    act.wait_ge(proj_done, 8 * i + m + 1)
                    if i:
                        act.wait_ge(glu_ready, m + 1)
                    A(sig[:, m, :], ps[:, 4 + m, :], ACT.Sigmoid).then_inc(sig_ready, 1)
                for s in range(1, 4):
                    first_high(2 * i + 1, s)
                for s in range(4):
                    first_high(2 * i + 2, s)
            for s in range(4):
                first_high(5, s)
            for s in range(4):
                first_high(6, s)

            for g in range(NG):
                W0 = 0 if g == 0 else P
                first_high(7 + 3 * g, 0)
                for t in range(TT):
                    act.wait_ge(proj_done, 16 + 12 * g + 8 + t + 1)
                    if g:
                        act.wait_ge(pv_done, HG * g)
                    A(v_sb[:, t, :], ps[:, 4 + t, :], ACT.Copy).then_inc(v_ready, 1)
                first_high(7 + 3 * g, 1)

                def exps(h):
                    H = HG * g + h
                    act.wait_ge(centred, H + 1)
                    A(sm[h % 2][:, :, W0:], sm[h % 2][:, :, W0:], ACT.Exp).then_inc(p_ready, 1)

                exps(0)
                for h in range(HG):
                    H = HG * g + h
                    act.wait_ge(pT_done, H + 1)
                    if H >= 2:
                        act.wait_ge(pv_done, H - 1)
                    T_ = psum[:, 2048:3072].rearrange("p (b k) -> p b k", b=8)
                    if g == 0:
                        A(probT[h % 2][:, 1:, :], T_[:, 1:, :], ACT.Copy).then_inc(pT_ready, 1)
                    else:
                        odd = T_.rearrange("p (b two) k -> p b two k", two=2)[:, :, 1, :]
                        A(probT[h % 2].rearrange("p (b two) k -> p b two k", two=2)[:, :, 1, :], odd, ACT.Copy).then_inc(pT_ready, 1)
                    if h + 1 < HG:
                        exps(h + 1)
                    act.wait_ge(pv_done, H + 1)
                    if g and h == 0:
                        act.wait_ge(o_stored, 16 * TT * g)
                    A(o_sb[:, :, h * DH:(h + 1) * DH], ps[:, 6 + h % 2, :].rearrange("p (b d) -> p b d", b=TT), ACT.Copy).then_inc(o_ready, 1)
                act.wait_ge(o_ready, HG * (g + 1))
                act.wait_ge(z_ready, HG * (g + 1))
                for b in range(TT):
                    rows = scr_o[g, b * P:(b + 1) * P, :] if g == 0 else scr_o[g].rearrange("(l r) c -> r l c", r=TT)[b]
                    nc.scalar.dma_start(rows, o_sb[:, b, :]).then_inc(o_stored, 16)
                if g < NG - 1:
                    first_high(7 + 3 * g, 2)
                    first_high(7 + 3 * g, 3)
                    for G in (8 + 3 * g, 9 + 3 * g):
                        for s in range(4):
                            first_high(G, s)

            act.wait_ge(o_stored, 16 * TT * NG)
            for g in range(NG):
                nc.scalar.dma_start(stats[:, :, g, :], scr_o[g].rearrange("(t p) c -> p t c", p=P)[:, :, HG * DH:]).then_inc(stats_in, 16)

            for t in range(TT):
                nc.scalar.dma_start(og[t], scr_o[:, t * P:(t + 1) * P, 0:HG * DH].rearrange("g p c -> p g c")).then_inc(og_in[t], 16)
            act.wait_ge(gap_ready, NG)
            A(coef, coef, ACT.Exp).then_inc(gexp_ready, 1)

            for c in range(CO):
                act.wait_ge(ln_centred, c + 1)
                A(sq[:, c, :], cv[:, c, :], ACT.Square).then_inc(ln_sq, 1)

            def gate_high(cg, s, first=False):
                later_high(s, 13 + 3 * cg, U_GATES if first else U_GATES - 2 + 8 * cg, U_GATES + 8 * cg,
                           52 if first else 44 + 16 * cg)

            def gate2_high(cg, s):
                later_high(s, 14 + 3 * cg, U_GATES + 3 + 8 * cg, U_GATES + 3 + 8 * cg, 56 + 16 * cg)

            def branch_gates(cg, first):
                for s in range(2 if first else 0, 4):
                    gate_high(cg, s, first)
                gate2_high(cg, 0)
                for m in range(4):
                    act.wait_ge(proj_done, 52 + 16 * cg + m + 1)
                    A(mixT[:, bass.ds(12 + m - 4 * cg, 1), :], ps[:, m, :], ACT.Sigmoid).then_inc(gate_sig, 1)
                gate2_high(cg, 1)
                if first:
                    act.wait_ge(ln_var, 1)
                    A(ln_std, ln_std, ACT.Sqrt).then_inc(ln_std_ready, 1)
                    for c in range(CO):
                        act.wait_ge(ln_norm, c + 1)
                        A(cv[:, c, :], cv[:, c, :], ACT.Silu, scale=sml[:, S_LG + c:S_LG + c + 1],
                          bias=sml[:, S_LB + c:S_LB + c + 1]).then_inc(convT_ready, 1)
                gate2_high(cg, 2)
                gate2_high(cg, 3)
                for m in range(4):
                    act.wait_ge(proj_done, 52 + 16 * cg + 4 + m + 1)
                    if not first:
                        act.wait_ge(mix_ready, 4 * cg)
                    A(sgc[:, m, :], ps[:, 4 + m, :], ACT.Sigmoid).then_inc(gate_sig, 1)
                if first:
                    for t in range(TT):
                        act.wait_ge(attnT_done, t + 1)
                        A(attnT[:, :, t * P:(t + 1) * P], ps[:, t, :].rearrange("p (h d) -> p h d", h=HG), ACT.Copy).then_inc(attnT_ready, 1)
                act.wait_ge(adaT_done, cg + 1)
                A(modc[:, bass.ds(cg, 1), :], ps[:, 4, 0:KT], ACT.Copy).then_inc(adaT_read, 1)

            branch_gates(0, True)
            with act.Fori(1, 4) as cg:
                branch_gates(cg, False)

            def out_high(n, s):
                later_high(s, 25 + n, U_OUT - 2 if n == 0 else U_OUT + 3 * n, U_OUT + 3 * n, 108 if n == 0 else 116 + 4 * n)

            def q_high(n, s):
                later_high(s, 29 + n, U_Q + 3 * n, U_Q + 3 * n, 132 + 4 * n)

            def mix_highs(ks):
                for k in ks:
                    act.wait_ge(mix_ready, k + 1)
                    A(x_high[:, k, :], mixT[:, mix_at(k), :], ACT.Copy).then_inc(mix_high, 1)

            act.wait_ge(proj_done, 108)
            mix_highs(range(12))
            out_high(0, 0)
            out_high(0, 1)
            mix_highs(range(12, KT))
            act.wait_ge(modr_done, 1)
            A(modr[0:4 * KT, :], ps[0:4 * KT, 0, 0:P], ACT.Copy).then_inc(modr_ready, 1)
            act.wait_ge(modr_ready, 1)
            nc.scalar.dma_start(scr_m.rearrange("j (k c) -> (j k) c", c=P), modr[0:4 * KT, :]).then_inc(modr_stored, 16)
            out_high(0, 2)
            out_high(0, 3)
            act.wait_ge(modr_stored, 16)
            act.wait_ge(mix_split, KT)
            act.wait_ge(proj_done, 116)
            for j, row in enumerate((rowG1, rowB2, rowA2)):
                nc.scalar.dma_start(row, scr_m[j:j + 1, :].to_broadcast([P, D])).then_inc(rows_in, 16)
            nc.scalar.dma_start(rowG3, scr_m[3:4, :].to_broadcast([P, D])).then_inc(g3_in, 16)

            def x_load(t):
                if t >= 2:
                    act.wait_ge(x2_stored[t % 2], 16)
                    act.wait_ge(h2_ready, t - 1)
                nc.scalar.dma_start(xb[t % 2], x[t * P:(t + 1) * P, :]).then_inc(xb_in[t % 2], 16)

            x_load(0)
            x_load(1)
            for n in range(4):
                half = n % 2
                next_high = (lambda s: out_high(n + 1, s)) if n < 3 else (lambda s: q_high(0, s))
                next_high(0)
                for t in range(TT):
                    act.wait_ge(proj_done, 116 + 4 * n + t + 1)
                    A(y_sb[:, t, n * NT:(n + 1) * NT], ps[:, 4 * half + t, :], ACT.Copy)
                    A(ps[:, 4 * half + t, :], ps[:, 4 * half + t, :], ACT.Square,
                      accum_out=ssqy[:, t, n:n + 1]).then_inc(y_ready, 1)
                for s in range(1, 4 if n < 3 else 2):
                    next_high(s)

            def x2_std(t):
                act.wait_ge(x2_ready, t + 1)
                nc.scalar.dma_start(scr_x[t, :, :], xb[t % 2]).then_inc(x2_stored[t % 2], 16)
                st.link(A(y_sb[:, t, :], xb[t % 2], ACT.Square, accum_out=ssq[:, TT + t:TT + t + 1]))
                A(std[:, TT + t:TT + t + 1], ssq[:, TT + t:TT + t + 1], ACT.Sqrt, scale=1.0 / D, bias=eps).then_inc(x2std_ready, 1)

            def h2T_high(t):
                for k4 in range(4):
                    act.wait_ge(h2T_done, 4 * t + k4 + 1)
                    A(x_high[:, 4 * k4:4 * k4 + 4, t * P:(t + 1) * P],
                      ps[:, 4 * (t % 2) + k4, :].rearrange("p (k c) -> p k c", k=4), ACT.Copy).then_inc(h2_high, 1)

            act.wait_ge(ysum_ready, 1)
            A(std[:, 0:TT], ssq[:, 0:TT], ACT.Sqrt, scale=1.0 / D, bias=eps).then_inc(ystd_ready, 1)
            x2_std(0)
            x2_std(1)
            x_load(2)
            x_load(3)
            h2T_high(0)
            x2_std(2)
            h2T_high(1)
            x2_std(3)
            h2T_high(2)
            act.wait_ge(h2_ready, TT)
            nc.scalar.dma_start(keys.rearrange("p k c -> p (k c)"), keysT).then_inc(keys_in, 16)
            h2T_high(3)

            def route_copies(n, first=False, last=False):
                q_high(n, 2)
                q_high(n, 3)
                if not last:
                    q_high(n + 1, 0)
                for m in range(4):
                    act.wait_ge(proj_done, 132 + 4 * n + m + 1)
                    if not first:
                        act.wait_ge(sc_done, 4 * n)
                    A(qs[:, m, :], ps[:, m, :], ACT.Copy).then_inc(q_ready, 1)
                if not last:
                    q_high(n + 1, 1)
                if n == 1:
                    for b in range(2):
                        act.wait_ge(x2_stored[b], 32)
                for m in range(4):
                    act.wait_ge(sc_done, 4 * n + m + 1)
                    A(sc[n][:, m, :, :], ps[:, 4 + m, :].rearrange("p (t k) -> p t k", t=TT), ACT.Copy).then_inc(sc_ready, 1)

            for n in range(4):
                route_copies(n, first=(n == 0), last=(n == 3))

            def gate_exp(t):
                act.wait_ge(gap2_ready, 4 * t + 4)
                tile = gate[:, bass.ds(t * PH * TK, PH * TK)]
                A(tile, tile, ACT.Exp).then_inc(exp2_ready, 1)

            gate_exp(0)
            act.wait_ge(q_ready, KT)
            act.wait_ge(sc_ready, KT)

            def load_h2p(t):
                A(h2p, h2[:, bass.ds(t, 1), :], ACT.Copy).then_inc(h2p_ready, 1)

            def unit(n, first=False):
                act.wait_ge(dots_done, TK * n + TK)
                A(gel, pre, ACT.Gelu).then_inc(gelu_ready, 1)
                act.wait_ge(act_ready, n + 1)
                for s in range(TK):
                    if not first:
                        act.wait_ge(u_used, TK * (n - 1) + s + 1)
                    A(diag[:, s, :], ident, ACT.Copy, scale=actv[:, s:s + 1]).then_inc(diag_ready, 1)

            def take_z(t):
                act.wait_ge(u_used, TK * PH * (t + 1))
                act.wait_ge(x2b_in, 16 * (t + 1))
                A(zs, zacc, ACT.Copy)
                A(zacc, zacc, ACT.Square, accum_out=zq[:, 0:1]).then_inc(z_read, 1)
                act.wait_ge(z_read, t + 1)
                A(zq[:, 1:2], zq[:, 0:1], ACT.Sqrt, scale=1.0 / D, bias=eps).then_inc(zstd_ready, 1)

            for b in range(2):
                act.wait_ge(x2_stored[b], 32)
            load_h2p(0)
            unit(0, True)
            with act.Fori(1, 6) as h:
                unit(h)
            gate_exp(1)
            unit(6)
            unit(7)
            with act.Fori(1, TT - 1) as t:
                act.wait_ge(dots_done, TK * PH * t)
                load_h2p(t)
                unit(PH * t)
                take_z(t - 1)
                with act.Fori(1, 6) as h:
                    unit(PH * t + h)
                gate_exp(t + 1)
                unit(PH * t + 6)
                unit(PH * t + 7)
            act.wait_ge(dots_done, TK * PH * (TT - 1))
            load_h2p(TT - 1)
            unit(PH * (TT - 1))
            take_z(TT - 2)
            with act.Fori(1, PH) as h:
                unit(PH * (TT - 1) + h)
            take_z(TT - 1)

        @block.vector
        def _(dve):
            st = Steps(dve, dve_step, passed_waits)
            V = nc.vector
            dve.wait_ge(consts_in, 32)
            dve.wait_ge(pos_in, 16)
            st.link(V.tensor_copy(rt1, cosT.bitcast(i32)))
            st.link(V.tensor_scalar(rt1, rt1, inv_freq, None, ALU.mult))
            st.link(V.tensor_scalar(rt2, rt1, 1.0 / TWO_PI, ROUND, ALU.mult, ALU.add))
            st.link(V.tensor_scalar(rt2, rt2, ROUND, None, ALU.subtract))
            for c in (PI_C1, PI_C2, PI_C3):
                st.link(V.scalar_tensor_tensor(rt1, rt2, -c, rt1, ALU.mult, ALU.add))
            st.link(V.tensor_scalar(rt2, rt1, TWO_PI / 4, None, ALU.add))
            st.link(V.tensor_scalar(cosT, rt2, TWO_PI / 2, -TWO_PI, ALU.is_gt, ALU.mult))
            st.link(V.tensor_tensor(rt2, rt2, cosT, ALU.add))
            st.link(V.tensor_scalar(rt1, rt1, PI, -PI, ALU.min, ALU.max))
            V.tensor_scalar(rt2, rt2, PI, -PI, ALU.min, ALU.max).then_inc(angle_ready, 1)

            dve.wait_ge(csil_ready, 1)

            def normalise():
                dve.wait_ge(std_ready, 1)
                st.link(V.reciprocal(rstd[:, 0:TT], std[:, 0:TT]))
                for t in range(TT):
                    V.tensor_scalar(xt[:, t, :], xt[:, t, :], rstd[:, t:t + 1], None, ALU.mult).then_inc(xn_ready, 1)

            for j in range(2):
                if j:
                    dve.wait_ge(modT_done, 1)
                for k in range(KT):
                    dve.wait_ge(ada_in[k % 4], 16 * (KT // 4 * j + k // 4 + 1))
                    if k == 0:
                        ins = V.tensor_scalar(acc, ring_flat[0], csil[:, 0:1], None, ALU.mult)
                    else:
                        ins = V.scalar_tensor_tensor(acc, ring_flat[k % 4], csil[:, k:k + 1], acc, ALU.mult, ALU.add)
                    ins.then_inc(ada_used, 1)
                    dve.wait_ge(ada_used, KT * j + k + 1)
                    if j == 0 and k == 10:
                        normalise()
            dve.wait_ge(modT_done, 1)
            st.link(V.tensor_tensor(colA, ps[:, 6, 0:KT], adab[:, 1, :], ALU.add))
            st.link(V.scalar_tensor_tensor(colA, colA, 1.0, gain[:, 0, :], ALU.add, ALU.mult))
            dve.wait_ge(modT_done, 2)
            V.tensor_tensor(colB, ps[:, 7, 0:KT], adab[:, 0, :], ALU.add).then_inc(ab_ready, 1)
            for k in range(KT):
                dve.wait_ge(h_high, k + 1)
                V.tensor_tensor(x_low[:, k, :], h_tmp[k % 2], x_high[:, k, :].bitcast(fp32), ALU.subtract).then_inc(hT_ready, 1)

            dve.wait_ge(trig_ready, 2)
            st.link(V.tensor_scalar(sinT, sinT, sgn, None, ALU.mult))
            st.link(V.memset(u[:, :, 0:CW - 1], 0.0))
            for i in range(2):
                for m in range(4):
                    dve.wait_ge(sig_ready, 4 * i + m + 1)
                    dve.wait_ge(proj_done, 8 * i + 4 + m + 1)
                    V.tensor_tensor(u[:, 4 * i + m, CW - 1:], ps[:, m, :], sig[:, m, :], ALU.mult).then_inc(glu_ready, 1)

            def conv_pair(c0):
                if c0:
                    dve.wait_ge(conv_ready, c0)
                last = {}
                for j in range(1, CW):
                    for c in (c0, c0 + 1):
                        total, tap, src = conv_sum[c - c0], sc_w[:, c, j:j + 1], u[:, c, j:j + S]
                        if j == 1:
                            last[c] = st.did(V.tensor_scalar(total, src, tap, sml[:, S_CB + c:S_CB + c + 1], ALU.mult, ALU.add))
                        else:
                            st.seen(last[c])
                            last[c] = st.did(V.scalar_tensor_tensor(total, src, tap, total, ALU.mult, ALU.add))
                for c in (c0, c0 + 1):
                    st.seen(last[c])
                    V.scalar_tensor_tensor(cv[:, c, :], cv[:, c, :], sc_w[:, c, 0:1], conv_sum[c - c0],
                                           ALU.mult, ALU.add).then_inc(conv_ready, 1)

            def rope(dst, g, h, bank, n):
                dve.wait_ge(proj_done, n)
                dil = DILATIONS[g]
                src = ps[:, bank, :]
                st.did(V.tensor_tensor(rt1, src, cosT, ALU.mult))
                st.did(V.tensor_tensor(rt2[0:64, :], src[64:128, :], sinT[0:64, :], ALU.mult))
                st.link(V.tensor_tensor(rt2[64:128, :], src[0:64, :], sinT[64:128, :], ALU.mult))
                o = dst[:, h, :]
                if dil == 1:
                    ins = V.tensor_tensor(o, rt1, rt2, ALU.add)
                else:
                    ins = V.tensor_tensor(o.rearrange("p (r l) -> p l r", r=TT), rt1.rearrange("p (l r) -> p l r", r=TT),
                                          rt2.rearrange("p (l r) -> p l r", r=TT), ALU.add)
                ins.then_inc(rope_ready, 1)
                return ins

            dve.wait_ge(glu_ready, 8)
            for g in range(NG):
                W0 = 0 if g == 0 else P
                for part, dst in ((0, q_sb), (1, k_sb)):
                    for h in range(HG):
                        n = 8 * g + 4 * part + h
                        if n:
                            dve.wait_ge(rope_ready, n)
                        rope(dst, g, h, 4 * (1 - part) + h, 16 + 12 * g + 4 * part + h + 1)
                    if g < 2:
                        conv_pair(4 * g + 2 * part)
                for h in range(HG):
                    H = HG * g + h
                    S_ = psum[:, 1024 * (h % 2):1024 * (h % 2) + 1024].rearrange("p (b k) -> p b k", b=TT)
                    dve.wait_ge(s_done, H + 1)
                    if H >= 2:
                        dve.wait_ge(pT_done, H - 1)
                    m_ = mask0 if g == 0 else mask1[g].unsqueeze(1).to_broadcast([P, TT, P])
                    part = sm[h % 2][:, :, W0:]
                    V.scalar_tensor_tensor(part, S_[:, :, W0:], SCALE, m_, ALU.mult, ALU.add).then_inc(s_read, 1)
                    dve.wait_ge(s_read, H + 1)
                    mx = o_sb[:, :, HG * DH + h]
                    if g and h == 0:
                        dve.wait_ge(o_stored, 16 * TT * g)
                    st.link(V.tensor_reduce(mx, part, AX, ALU.max))
                    V.tensor_tensor(part, part, mx.unsqueeze(2).to_broadcast([P, TT, 2 * P - W0]), ALU.subtract).then_inc(centred, 1)
                    dve.wait_ge(p_ready, H + 1)
                    V.tensor_reduce(o_sb[:, :, HG * DH + HG + h], part, AX, ALU.add).then_inc(z_ready, 1)

            dve.wait_ge(lnsum_done, 1)
            for c in range(CO):
                V.scalar_tensor_tensor(cv[:, c, :], ps[:, 7, :], -1.0 / CC, cv[:, c, :], ALU.mult, ALU.add).then_inc(ln_centred, 1)

            dve.wait_ge(stats_in, 16 * NG)
            mx_ = stats[:, :, :, 0:HG]
            zz_ = stats[:, :, :, HG:]
            st.link(V.tensor_tensor(stat_m, mx_[:, :, 0, :], mx_[:, :, 1, :], ALU.max))
            st.link(V.tensor_tensor(stat_m, stat_m, mx_[:, :, 2, :], ALU.max))
            for g in range(NG):
                V.tensor_tensor(coef[:, :, g, :], mx_[:, :, g, :], stat_m, ALU.subtract).then_inc(gap_ready, 1)
            dve.wait_ge(gexp_ready, 1)
            st.link(V.tensor_tensor(zz_, zz_, coef, ALU.mult))
            st.link(V.tensor_tensor(stat_d, zz_[:, :, 0, :], zz_[:, :, 1, :], ALU.add))
            st.link(V.tensor_tensor(stat_d, stat_d, zz_[:, :, 2, :], ALU.add))
            st.link(V.reciprocal(stat_d, stat_d))
            for g in range(NG):
                st.did(V.tensor_tensor(coef[:, :, g, :], coef[:, :, g, :], stat_d, ALU.mult))
            st.seen(st.n)

            dve.wait_ge(lnsq_done, 1)
            V.tensor_scalar(ln_std, ps[:, 7, :], 1.0 / CC, EPS, ALU.mult, ALU.add).then_inc(ln_var, 1)
            dve.wait_ge(ln_std_ready, 1)
            st.link(V.reciprocal(ln_r, ln_std))
            for c in range(CO):
                V.tensor_tensor(cv[:, c, :], cv[:, c, :], ln_r, ALU.mult).then_inc(ln_norm, 1)
            for t in range(TT):
                dve.wait_ge(og_in[t], 16)
                for g in range(NG):
                    for h in range(HG):
                        part = og[t][:, g, h * DH:(h + 1) * DH]
                        dst = og[t][:, 0, h * DH:(h + 1) * DH]
                        cf = coef[:, t, g, h:h + 1]
                        if g == 0:
                            ins = V.tensor_scalar(dst, part, cf, None, ALU.mult)
                        else:
                            dve.wait_ge(og_used, HG * (NG * t + g - 1) + h + 1)
                            ins = V.scalar_tensor_tensor(dst, part, cf, dst, ALU.mult, ALU.add)
                        ins.then_inc(og_used, 1)

            def branch(cg, first):
                if not first:
                    dve.wait_ge(adaT_done, cg)
                for j in range(2 * KT):
                    k, s = j // 2, j % 2
                    dve.wait_ge(ada2_in[s], 16 * (KT * cg + k + 1))
                    half = acc[:, s * (D // 2):(s + 1) * (D // 2)]
                    if k == 0:
                        ins = V.tensor_scalar(half, ada_ring[s], csil[:, 0:1], None, ALU.mult)
                    else:
                        dve.wait_ge(ada2_used, 2 * KT * cg + j - 1)
                        ins = V.scalar_tensor_tensor(half, ada_ring[s], csil[:, k:k + 1], half, ALU.mult, ALU.add)
                    ins.then_inc(ada2_used, 1)
                for b in range(2):
                    for m in range(4):
                        dve.wait_ge(gate_sig, 8 * cg + 4 * b + m + 1)
                        hold(dve, proj_done, 52 + 16 * cg + 8 + 4 * b + m + 1, passed_waits)
                        sg = sgc[:, m, :] if b else mixT[:, bass.ds(12 + m - 4 * cg, 1), :]
                        V.tensor_tensor(sg, sg, ps[:, 4 * b + m, :], ALU.mult).then_inc(branch_done, 1)
                for m in range(4):
                    hold(dve, branch_done, 8 * cg + 4 + m + 1, passed_waits)
                    mixed = mixT[:, bass.ds(12 + m - 4 * cg, 1), :]
                    V.tensor_tensor(mixed, mixed, sgc[:, m, :], ALU.add).then_inc(mix_ready, 1)

            branch(0, True)
            with dve.Fori(1, 4) as cg:
                branch(cg, False)

            dve.wait_ge(adaT_read, 4)
            st.link(V.tensor_tensor(modc, modc, adab[:, 2:6, :], ALU.add))
            st.did(V.tensor_tensor(modc[:, 0, :], modc[:, 0, :], gain[:, 1, :], ALU.mult))
            st.did(V.scalar_tensor_tensor(modc[:, 2, :], modc[:, 2, :], 1.0, gain[:, 2, :], ALU.add, ALU.mult))
            V.tensor_tensor(modc[:, 3, :], modc[:, 3, :], gain[:, 3, :], ALU.mult).then_inc(modc_ready, 1)

            def residual(t):
                dve.wait_ge(xb_in[t % 2], 16 * (t // 2 + 1))
                st.link(V.scalar_tensor_tensor(y_sb[:, t, :], y_sb[:, t, :], rstd[:, t:t + 1], rowG1, ALU.mult, ALU.mult))
                V.tensor_tensor(xb[t % 2], xb[t % 2], y_sb[:, t, :], ALU.add).then_inc(x2_ready, 1)

            def modulated(t):
                dve.wait_ge(x2std_ready, t + 1)
                st.link(V.reciprocal(rstd[:, TT + t:TT + t + 1], std[:, TT + t:TT + t + 1]))
                st.link(V.scalar_tensor_tensor(h2[:, t, :], xb[t % 2], rstd[:, TT + t:TT + t + 1], rowA2, ALU.mult, ALU.mult))
                V.tensor_tensor(h2[:, t, :], h2[:, t, :], rowB2, ALU.add).then_inc(h2_ready, 1)

            def h2T_low(t):
                for k4 in range(4):
                    dve.wait_ge(h2_high, 4 * t + k4 + 1)
                    at = (slice(None), slice(4 * k4, 4 * k4 + 4), slice(t * P, (t + 1) * P))
                    V.tensor_tensor(x_low[at], ps[:, 4 * (t % 2) + k4, :].rearrange("p (k c) -> p k c", k=4),
                                    x_high[at].bitcast(fp32), ALU.subtract).then_inc(h2T_ready, 1)

            dve.wait_ge(y_ready, 16)
            V.tensor_reduce(ssq[:, 0:TT], ssqy, AX, ALU.add).then_inc(ysum_ready, 1)
            dve.wait_ge(ystd_ready, 1)
            dve.wait_ge(rows_in, 48)
            st.link(V.reciprocal(rstd[:, 0:TT], std[:, 0:TT]))
            residual(0)
            residual(1)
            modulated(0)
            modulated(1)
            h2T_low(0)
            residual(2)
            residual(3)
            h2T_low(1)
            modulated(2)
            modulated(3)
            h2T_low(2)
            h2T_low(3)

            def top16(vals, inds, src, count):
                for i in range(count):
                    st.did(V.max(vals[:, i, 0:8], src[:, i, :]))
                st.seen(st.off + st.n)
                for i in range(count):
                    st.did(V.max_index(inds[:, i, 0:8], vals[:, i, 0:8], src[:, i, :]))
                st.seen(st.off + st.n)
                for i in range(count):
                    st.did(V.match_replace(src[:, i, :], vals[:, i, 0:8], src[:, i, :], LOWEST))
                st.seen(st.off + st.n)
                for i in range(count):
                    st.did(V.max(vals[:, i, 8:16], src[:, i, :]))
                st.seen(st.off + st.n)
                for i in range(count):
                    st.did(V.max_index(inds[:, i, 8:16], vals[:, i, 8:16], src[:, i, :]))
                st.seen(st.off + st.n)

            def route(t, n):
                st.link(V.tensor_copy(sc_part.unsqueeze(2), sc[n][:, :, bass.ds(t, 1), :]))
                top16(v12, i12, sc_part, HG)
                st.did(V.tensor_copy(i12f, i12))
                for hh in range(2):
                    a_ = v12[:, 2 * hh, :].unsqueeze(2).to_broadcast([P, TK, TK])
                    b_ = v12[:, 2 * hh + 1, :].unsqueeze(1).to_broadcast([P, TK, TK])
                    st.did(V.tensor_tensor(cand[:, hh, :].rearrange("p (a b) -> p a b", a=TK), a_, b_, ALU.add))
                st.seen(st.off + st.n)
                top16(top, topi, cand, 2)
                def of_heads(x_):
                    return x_.rearrange("p (t h s) -> p t h s", t=TT, h=PH)[:, bass.ds(t, 1), 2 * n:2 * n + 2, :]

                V.tensor_tensor(of_heads(gate), top.unsqueeze(1), top[:, :, 0:1].unsqueeze(1).to_broadcast([P, 1, 2, TK]),
                                ALU.subtract).then_inc(gap2_ready, 1)
                st.did(V.tensor_scalar(pair[:, :, 0, :], topi, 4, None, ALU.logical_shift_right))
                st.link(V.tensor_scalar(pair[:, :, 1, :], topi, TK - 1, None, ALU.bitwise_and))
                st.link(V.tensor_copy(pairf, pair.rearrange("p h b s -> p (h b s)")))
                st.link(V.tensor_tensor(hot, pairf.unsqueeze(2).to_broadcast([P, 4 * TK, TK]),
                                        iota.unsqueeze(1).to_broadcast([P, 4 * TK, TK]), ALU.is_equal))
                hot4 = hot.rearrange("p (m s) a -> p m s a", m=HG)
                st.link(V.tensor_tensor(hot4, hot4, i12f.unsqueeze(2).to_broadcast([P, HG, TK, TK]), ALU.mult))
                st.link(V.tensor_reduce(picked.rearrange("p h b s -> p (h b s)"), hot, AX, ALU.add))
                V.scalar_tensor_tensor(of_heads(idx), picked[:, :, 0, :].unsqueeze(1), float(P), picked[:, :, 1, :].unsqueeze(1),
                                       ALU.mult, ALU.add).then_inc(routed, 2)

            def softmax(t):
                hold(dve, exp2_ready, t + 1, passed_waits)
                g_ = gate.rearrange("p (t h s) -> p t h s", t=TT, h=PH)[:, bass.ds(t, 1), :, :]
                st.link(V.tensor_reduce(den.unsqueeze(1), g_, AX, ALU.add))
                st.link(V.reciprocal(rden, den))
                st.link(V.tensor_tensor(g_, g_, rden.unsqueeze(1).unsqueeze(3).to_broadcast([P, 1, PH, TK]), ALU.mult))

            for n in range(4):
                dve.wait_ge(sc_ready, 4 * n + 4)
                route(0, n)
            softmax(0)

            def unit(n, first=False):
                for s in range(TK):
                    dve.wait_ge(d_in[s % NB], 16 * (2 * n + s // NB + 1))
                    row = d_row[s % NB]
                    V.tensor_tensor_reduce(row, row, h2p, 1.0, 0.0, ALU.mult, ALU.add, pre[:, s:s + 1]).then_inc(dots_done, 1)
                dve.wait_ge(gelu_ready, n + 1)
                if not first:
                    dve.wait_ge(diag_ready, TK * n)
                V.tensor_tensor(actv, gel, gate[:, bass.ds(n * TK, TK)], ALU.mult).then_inc(act_ready, 1)

            def finish(t):
                dve.wait_ge(zstd_ready, t + 1)
                dve.wait_ge(x2b_in, 16 * (t + 1))
                st.link(V.reciprocal(zq[:, 2:3], zq[:, 1:2]))
                st.link(V.scalar_tensor_tensor(zs, zs, zq[:, 2:3], rowG3, ALU.mult, ALU.mult))
                V.tensor_tensor(zs, zs, x2b, ALU.add).then_inc(out_ready, 1)

            def tile_rest(t, route_next):
                for n in range(4):
                    unit(PH * t + 2 + n)
                    if route_next:
                        route(t + 1, n)
                unit(PH * t + 6)
                if route_next:
                    softmax(t + 1)
                unit(PH * t + 7)

            dve.wait_ge(g3_in, 16)
            dve.wait_ge(h2p_ready, 1)
            unit(0, True)
            unit(1)
            tile_rest(0, True)
            with dve.Fori(1, TT - 1) as t:
                st.enter(t - 1, TILE_STEPS)
                hold(dve, h2p_ready, t + 1, passed_waits)
                unit(PH * t)
                unit(PH * t + 1)
                finish(t - 1)
                tile_rest(t, True)
                st.leave(TT - 2)
            dve.wait_ge(h2p_ready, TT)
            unit(PH * (TT - 1))
            unit(PH * (TT - 1) + 1)
            finish(TT - 2)
            with dve.Fori(2, PH) as h:
                unit(PH * (TT - 1) + h)
            finish(TT - 1)


_OUT = ((1, S, D), "float32")


def constants():
    import numpy as np
    c = np.zeros((P, C_END), np.float32)
    c[:, C_ID:C_ID + P] = np.eye(P)
    c[:, C_ONE:C_ONE + P] = 1.0
    q = np.arange(P)[:, None]
    k = np.arange(P)[None, :]
    m0 = np.zeros((P, TT, 2 * P), np.float32)
    m0[:, :, :P] = np.where(k >= q, 0.0, MASK)[:, None, :]
    m0[:, 0, :P] = MASK
    m0[:, :, P:] = np.where(k <= q, 0.0, MASK)[:, None, :]
    c[:, C_M0:C_M0 + TT * 2 * P] = m0.reshape(P, -1)
    c[:, C_M1:C_M1 + P] = np.where(k <= q, 0.0, MASK)
    c[:, C_M2:C_M2 + P] = np.where((k <= q) & (k % 4 == q % 4), 0.0, MASK)
    inv = np.float32(10000.0) ** (-np.arange(0, DH, 2, dtype=np.float32) / np.float32(DH))
    c[:, C_INV] = np.concatenate([inv, inv])
    c[:, C_SGN] = np.where(np.arange(P) < 64, -1.0, 1.0)
    c[:, C_EPS] = EPS
    c[:, C_IOTA:C_IOTA + TK] = np.arange(TK)
    return c


def kernel(x, c, positions, ada_w, ada_b, norm_gains, w_in, w_attn_o, conv_w, conv_b, conv_ln_g, conv_ln_b,
           w_conv_o, w_out, peer_w_q, peer_sub_keys, peer_down, peer_up):
    import numpy as np
    import concourse.bacc as bacc
    from concourse.bass_utils import run_bass_kernel_spmd

    def columns(a, n):
        return np.asarray(a).reshape(n, P).T

    small = np.concatenate([
        columns(c, KT), columns(ada_b, 6 * KT), columns(norm_gains, 4 * KT), columns(conv_b, CO),
        columns(conv_ln_g, CO), columns(conv_ln_b, CO),
        np.asarray(conv_w).reshape(CW, CO, P).transpose(2, 1, 0).reshape(P, CO * CW)], axis=1)
    keysT = np.asarray(peer_sub_keys).reshape(2 * PH, P, P).transpose(2, 0, 1).reshape(P, 2 * PH * P)
    ins = {
        "x": np.asarray(x)[0], "ada_w": np.asarray(ada_w)[0], "w_in": np.asarray(w_in)[0],
        "w_attn_o": np.asarray(w_attn_o)[0], "w_conv_o": np.asarray(w_conv_o)[0], "w_out": np.asarray(w_out)[0],
        "w_q": np.asarray(peer_w_q)[0], "down": np.asarray(peer_down)[0], "up": np.asarray(peer_up)[0],
        "keysT": keysT, "pos": np.asarray(positions), "small": small, "const": constants(),
    }
    nc = bacc.Bacc("TRN2", target_bir_lowering=False, num_devices=1)
    arrays, args = {}, []
    for name, a in ins.items():
        arrays[f"in_{name}"] = np.ascontiguousarray(a)
        args.append(nc.dram_tensor(f"in_{name}", a.shape, mybir.dt.from_np(a.dtype), kind="ExternalInput").ap())
    out = nc.dram_tensor("out_0", (S, D), mybir.dt.float32, kind="ExternalOutput").ap()
    block_kernel(nc, *args, out)
    r = run_bass_kernel_spmd(nc, [arrays], core_ids=[0])
    return r.results[0]["out_0"].reshape(1, S, D)
```
